# Optimizing a Trainium2 kernel written in Bass

```python
import math
import jax, jax.numpy as jnp
from jax import lax
import numpy as np

D_MODEL = 2048
BATCH = 1
SEQ = 512
DEPTH = 1

MIX_WIDTH = D_MODEL
ATTN_WIDTH = MIX_WIDTH // 2
POOL_WIDTH = MIX_WIDTH - ATTN_WIDTH
HEAD_DIM = 64
N_ATTN_HEADS = ATTN_WIDTH // (2 * HEAD_DIM)
ROT_DIM = HEAD_DIM // 4
ROPE_THETA = 500000.0
POOL_WINDOWS = (2, 4, 8, 16)
N_POOL_GROUPS = len(POOL_WINDOWS)
POOL_GROUP = POOL_WIDTH // N_POOL_GROUPS
IN_WIDTH = 4 * ATTN_WIDTH + 2 * POOL_WIDTH
Q_BLOCK = 128
EPS = 1e-6

kernel_name = 'hybrid_diffattn_pool_block'

def lambda_init(layer_idx):
    return 0.8 - 0.6 * math.exp(-0.3 * (layer_idx - 1))

def rms_norm(x, w):
    xf = x.astype(jnp.float32)
    y = xf * lax.rsqrt(jnp.mean(xf * xf, axis=-1, keepdims=True) + EPS)
    return (y * w.astype(jnp.float32)).astype(x.dtype)

def rope_partial(t, cos, sin):
    half = ROT_DIM // 2
    tf = t.astype(jnp.float32)
    t1 = tf[..., :half]
    t2 = tf[..., half:ROT_DIM]
    out = jnp.concatenate([t1 * cos - t2 * sin, t2 * cos + t1 * sin, tf[..., ROT_DIM:]], axis=-1)
    return out.astype(t.dtype)

def diff_attention(q, k, v, q_norm_w, k_norm_w, lq1, lk1, lq2, lk2, subln_w, lam_init):
    B, S, _ = q.shape
    H, d = N_ATTN_HEADS, HEAD_DIM
    q = rms_norm(q.reshape(B, S, H, 2, d), q_norm_w)
    k = rms_norm(k.reshape(B, S, H, 2, d), k_norm_w)
    pos = jnp.arange(S, dtype=jnp.float32)
    inv_freq = ROPE_THETA ** (-jnp.arange(0, ROT_DIM, 2, dtype=jnp.float32) / ROT_DIM)
    ang = pos[:, None] * inv_freq[None, :]
    cos = jnp.cos(ang)[None, :, None, None, :]
    sin = jnp.sin(ang)[None, :, None, None, :]
    q = rope_partial(q, cos, sin)
    k = rope_partial(k, cos, sin)
    vh = v.reshape(B, S, H, 2 * d).transpose(0, 2, 1, 3)
    kt = k.transpose(0, 2, 3, 1, 4)
    nb = S // Q_BLOCK
    qb = q.reshape(B, nb, Q_BLOCK, H, 2, d).transpose(1, 0, 3, 4, 2, 5)
    f32 = jnp.float32
    lam = (jnp.exp(jnp.sum(lq1.astype(f32) * lk1.astype(f32)))
           - jnp.exp(jnp.sum(lq2.astype(f32) * lk2.astype(f32))) + lam_init)
    scale = 1.0 / math.sqrt(d)

    def block(qblk):
        s = jnp.einsum('bhcqd,bhckd->bhcqk', qblk, kt).astype(f32) * scale
        p = jax.nn.softmax(s, axis=-1)
        a = p[:, :, 0] - lam * p[:, :, 1]
        return jnp.einsum('bhqk,bhke->bhqe', a.astype(vh.dtype), vh)

    o = lax.map(block, qb)
    o = o.transpose(1, 0, 3, 2, 4).reshape(B, S, H, 2 * d)
    o = rms_norm(o, subln_w) * (1.0 - lam_init)
    return o.reshape(B, S, ATTN_WIDTH)

def centred_mean(u, w):
    B, S, C = u.shape
    lo = w // 2
    hi = w - 1 - lo
    up = jnp.pad(u.astype(jnp.float32), ((0, 0), (lo + 1, hi), (0, 0)))
    c = lax.cumsum(up, axis=1)
    total = c[:, w:w + S] - c[:, :S]
    pos = jnp.arange(S)
    cnt = (jnp.minimum(pos + hi, S - 1) - jnp.maximum(pos - lo, 0) + 1).astype(jnp.float32)
    return total / cnt[None, :, None]

def multiscale_pool(u, w_pool, pool_scale):
    B, S, _ = u.shape
    ug = u.reshape(B, S, N_POOL_GROUPS, POOL_GROUP)
    diffs = [centred_mean(ug[:, :, g], w) - ug[:, :, g].astype(jnp.float32)
             for g, w in enumerate(POOL_WINDOWS)]
    dg = jnp.stack(diffs, axis=2).astype(u.dtype)
    y = jnp.einsum('bsgc,gcd->bsgd', dg, w_pool).reshape(B, S, POOL_WIDTH)
    return y * pool_scale

def setup_inputs(seed: int = 0) -> dict:
    key = jax.random.key(seed)
    ks = jax.random.split(key, 14)
    nrm = jax.random.normal
    f32 = jnp.float32
    x = nrm(ks[0], (BATCH, SEQ, D_MODEL), f32)
    norm_w = 1.0 + 0.02 * nrm(ks[1], (DEPTH, D_MODEL), f32)
    w_in = nrm(ks[2], (DEPTH, D_MODEL, IN_WIDTH), f32) * D_MODEL ** -0.5
    q_norm_w = 1.0 + 0.02 * nrm(ks[3], (DEPTH, HEAD_DIM), f32)
    k_norm_w = 1.0 + 0.02 * nrm(ks[4], (DEPTH, HEAD_DIM), f32)
    lambda_q1 = 0.1 * nrm(ks[5], (DEPTH, HEAD_DIM), f32)
    lambda_k1 = 0.1 * nrm(ks[6], (DEPTH, HEAD_DIM), f32)
    lambda_q2 = 0.1 * nrm(ks[7], (DEPTH, HEAD_DIM), f32)
    lambda_k2 = 0.1 * nrm(ks[8], (DEPTH, HEAD_DIM), f32)
    subln_w = 1.0 + 0.02 * nrm(ks[9], (DEPTH, 2 * HEAD_DIM), f32)
    w_pool = nrm(ks[10], (DEPTH, N_POOL_GROUPS, POOL_GROUP, POOL_GROUP), f32) * POOL_GROUP ** -0.5
    pool_scale = 1.0 + 0.02 * nrm(ks[11], (DEPTH, POOL_WIDTH), f32)
    w_out = nrm(ks[12], (DEPTH, MIX_WIDTH, D_MODEL), f32) * MIX_WIDTH ** -0.5
    return {'x': x, 'norm_w': norm_w, 'w_in': w_in, 'q_norm_w': q_norm_w, 'k_norm_w': k_norm_w,
            'lambda_q1': lambda_q1, 'lambda_k1': lambda_k1, 'lambda_q2': lambda_q2, 'lambda_k2': lambda_k2,
            'subln_w': subln_w, 'w_pool': w_pool, 'pool_scale': pool_scale, 'w_out': w_out}

def reference(x, norm_w, w_in, q_norm_w, k_norm_w, lambda_q1, lambda_k1, lambda_q2, lambda_k2,
              subln_w, w_pool, pool_scale, w_out):
    A, P = ATTN_WIDTH, POOL_WIDTH
    for l in range(DEPTH):
        h = rms_norm(x, norm_w[l])
        proj = h @ w_in[l]
        q, k, v, g_a, u_p, g_p = jnp.split(proj, [A, 2 * A, 3 * A, 4 * A, 4 * A + P], axis=-1)
        attn = diff_attention(q, k, v, q_norm_w[l], k_norm_w[l], lambda_q1[l], lambda_k1[l],
                              lambda_q2[l], lambda_k2[l], subln_w[l], lambda_init(l + 1))
        pool = multiscale_pool(u_p, w_pool[l], pool_scale[l])
        mixed = jnp.concatenate([attn * jax.nn.silu(g_a), pool * jax.nn.silu(g_p)], axis=-1)
        x = x + mixed @ w_out[l]
    return x


_drawn_inputs = setup_inputs


def setup_inputs(seed=0):
    import zlib

    import numpy as np

    out = dict(_drawn_inputs(seed))
    spreads = {}
    factors = {'norm_w': 3.41,
     'q_norm_w': 7.305,
     'k_norm_w': 8.0,
     'lambda_q1': 8.0,
     'lambda_q2': 3.2,
     'lambda_k2': 4.922,
     'subln_w': 8.0,
     'pool_scale': 8.0}
    for name, (base, spread) in spreads.items():
        noise = np.random.default_rng([zlib.crc32(name.encode()), seed]).standard_normal(out[name].shape)
        drawn = base * np.exp(spread * noise) if base else spread * noise
        out[name] = __import__('jax').numpy.asarray(drawn.astype(out[name].dtype))
    for name, factor in factors.items():
        out[name] = (out[name] * factor).astype(out[name].dtype)
    return out
```

```python
import math
from contextlib import ExitStack

import concourse.bass as bass
from concourse import mybir

F32 = mybir.dt.float32
F32R = mybir.dt.float32r
ALU = mybir.AluOpType
ACT = mybir.ActivationFunctionType
AX_X = mybir.AxisListType.X

P = 128
HEAD_DIM = 64
N_WINDOWS = 4
EPS = 1e-6
LAMBDA_INIT = 0.2
PAD = 8
RAW_SLOTS = 4
W_SLOTS = 4


def hybrid_block(nc, x, norm_w, w_in, q_norm_w, k_norm_w, lq1, lk1, lq2, lk2, subln_w, w_pool,
                 pool_scale, w_out, identity, pair_ones, rope_cos, rope_sin, inv_count, out):
    SEQ, D = x.shape
    KT = D // P
    ST = SEQ // P
    A = w_in.shape[1] // 6
    GC = 256
    ROUNDS = A // GC
    UNITS, HALVES = 24, 48
    G_UNITS, G_HALVES = 4, 8
    IN_HALVES = ROUNDS * HALVES
    NC = 512
    CHUNKS = D // NC
    C_UNITS, C_HALVES = KT // 2, KT
    START = 1
    CREDIT = ST + START
    ITEMS = 2 * ST
    SCALE = 1.0 / math.sqrt(HEAD_DIM)
    XW = SEQ + 2 * PAD
    Q, K, V, GA, U, GP = range(6)

    with ExitStack() as ctx:
        def sb(name, shape, dt=F32):
            return ctx.enter_context(nc.sbuf_tensor(name, shape, dt))

        def sem(name):
            return ctx.enter_context(nc.semaphore(name))

        h_hi = sb("h_hi", [P, KT, SEQ], F32R)
        h_lo = sb("h_lo", [P, KT, SEQ], F32R)
        mixed = sb("mixed", [P, KT * SEQ])
        raw = sb("raw", [P, RAW_SLOTS, 1024])
        w_hi = sb("w_hi", [P, W_SLOTS, 512], F32R)
        w_lo = sb("w_lo", [P, W_SLOTS, 512], F32R)
        q_hi = sb("q_hi", [P, 2, SEQ], F32R)
        q_lo = sb("q_lo", [P, 2, SEQ], F32R)
        k_hi = sb("k_hi", [P, 2, SEQ], F32R)
        k_lo = sb("k_lo", [P, 2, SEQ], F32R)
        work = sb("work", [P, 5 * 2 * XW])
        v_hi = sb("v_hi", [P, 2, SEQ], F32R)
        v_lo = sb("v_lo", [P, 2, SEQ], F32R)
        probs = sb("probs", [P, 2, SEQ])
        at_hi = sb("at_hi", [P, ST, SEQ], F32R)
        at_lo = sb("at_lo", [P, ST, SEQ], F32R)
        head_out = sb("head_out", [P, SEQ])
        gate = sb("gate", [P, 2, SEQ])
        wp_raw = sb("wp_raw", [P, 512])
        inv_cnt = sb("inv_cnt", [P, SEQ])
        cos_t = sb("cos_t", [P, SEQ])
        sin_t = sb("sin_t", [P, SEQ])
        ident = sb("ident", [P, P])
        ones_pair = sb("ones_pair", [P, P])
        ones_all = sb("ones_all", [P, P])
        qw = sb("qw", [P, 1])
        kw = sb("kw", [P, 1])
        sw = sb("sw", [P, 1])
        eps_t = sb("eps_t", [P, 1])
        p_scale = sb("p_scale", [P, 2])
        lam_in = sb("lam_in", [P, 4, HEAD_DIM])
        lam_prod = sb("lam_prod", [P, 2, HEAD_DIM])
        lam_sum = sb("lam_sum", [P, 2])
        lam_exp = sb("lam_exp", [P, 2])
        neg_lam = sb("neg_lam", [P, 1])
        x_ss = sb("x_ss", [P, ST])
        x_rms = sb("x_rms", [P, ST])
        x_rstd = sb("x_rstd", [P, ST])
        row_max = sb("row_max", [P, 2])
        neg_max = sb("neg_max", [P, 2])
        row_sum = sb("row_sum", [P, 2])
        row_inv = sb("row_inv", [P, 2])
        coef = sb("coef", [P, 1])

        ps = ctx.enter_context(nc.psum_tensor("ps", [P, 8, 512], F32))
        S0, TB, OB = 4, 6, 7

        x_rows = mixed[:, :].rearrange("p (t n) -> p t n", t=ST)
        norm_row = work[:, 0:D]

        def wk(i):
            return work[:, i * 2 * XW:(i + 1) * 2 * XW].rearrange("p (c n) -> p c n", c=2)[:, :, PAD:PAD + SEQ]

        def wk_cols(i, a, b):
            return work[:, i * 2 * XW:(i + 1) * 2 * XW].rearrange("p (c n) -> p c n", c=2)[:, :, a:b]

        def twice(t):
            return t[:, :].unsqueeze(1).to_broadcast([P, 2, SEQ])

        const_in = sem("const_in")
        lam_loaded = sem("lam_loaded")
        norm_row_in = sem("norm_row_in")
        x_in = [sem(f"x_in{i}") for i in range(ST)]
        x_squared, x_rms_ready, x_normed = sem("x_squared"), sem("x_rms_ready"), sem("x_normed")
        x_transposed, h_hi_ready, h_lo_ready = sem("x_transposed"), sem("h_hi_ready"), sem("h_lo_ready")
        setup_step, lam_summed, lam_exped = sem("setup_step"), sem("lam_summed"), sem("lam_exped")
        raw_in = [sem(f"raw_in{i}") for i in range(RAW_SLOTS)]
        w_hi_ready, w_lo_ready, w_used = sem("w_hi_ready"), sem("w_lo_ready"), sem("w_used")
        wp_in, inv_in, scale_in = sem("wp_in"), sem("inv_in"), sem("scale_in")
        squares_ready, squares_summed, log_ready, rstd_ready = (
            sem("squares_ready"), sem("squares_summed"), sem("log_ready"), sem("rstd_ready"))
        qk_normed, dve_step = sem("qk_normed"), sem("dve_step")
        qk_rotated, qk_hi_ready, qk_lo_ready = sem("qk_rotated"), sem("qk_hi_ready"), sem("qk_lo_ready")
        evacuated = sem("evacuated")
        v_transposed, v_hi_ready, v_lo_ready = sem("v_transposed"), sem("v_hi_ready"), sem("v_lo_ready")
        scored, max_ready, exp_done, attn_ready = sem("scored"), sem("max_ready"), sem("exp_done"), sem("attn_ready")
        at_transposed, at_hi_ready, at_lo_ready = sem("at_transposed"), sem("at_hi_ready"), sem("at_lo_ready")
        head_done, head_normed, head_mixed = sem("head_done"), sem("head_normed"), sem("head_mixed")
        wp_hi_ready, wp_lo_ready = sem("wp_hi_ready"), sem("wp_lo_ready")
        diff_ready, diff_hi_ready, diff_lo_ready = sem("diff_ready"), sem("diff_hi_ready"), sem("diff_lo_ready")
        pool_done, pool_mixed = sem("pool_done"), sem("pool_mixed")
        m_hi_ready, m_lo_ready = sem("m_hi_ready"), sem("m_lo_ready")
        res_in = [sem(f"res_in{i}") for i in range(CHUNKS)]
        out_tile_done, out_added, out_stored = sem("out_tile_done"), sem("out_added"), sem("out_stored")

        w_in_rows = w_in.rearrange("(k p) n -> p k n", p=P)
        w_out_rows = w_out.rearrange("(k p) n -> p k n", p=P)
        x_tiles = x.rearrange("(t p) n -> p t n", p=P)
        out_tiles = out.rearrange("(t p) n -> p t n", p=P)

        block = ctx.enter_context(nc.Block())

        @block.sync
        def _(sp):
            sp.dma_start(norm_row, norm_w.to_broadcast([P, D])).then_inc(norm_row_in, 16)
            for t in range(ST):
                sp.dma_start(x_rows[:, t, :], x_tiles[:, t, :]).then_inc(x_in[t], 16)

            def load_in(unit, rnd):
                g, j = divmod(unit, G_UNITS)
                sp.dma_start(raw[:, unit % RAW_SLOTS, :].rearrange("p (k n) -> p k n", k=4),
                             w_in_rows[:, 4 * j:4 * j + 4, bass.ds(rnd * GC + g * A, GC)]
                             ).then_inc(raw_in[unit % RAW_SLOTS], 16)

            def load_out(j, chunk):
                sp.dma_start(raw[:, j % RAW_SLOTS, :].rearrange("p (k n) -> p k n", k=2),
                             w_out_rows[:, 2 * j:2 * j + 2, bass.ds(chunk * NC, NC)]
                             ).then_inc(raw_in[j % RAW_SLOTS], 16)

            for unit in range(RAW_SLOTS):
                load_in(unit, 0)
            with sp.Fori(0, ROUNDS - 1) as r:
                for unit in range(UNITS):
                    sp.wait_ge(w_lo_ready, r * HALVES + 2 * unit + 2)
                    nxt = unit + RAW_SLOTS
                    if nxt < UNITS:
                        load_in(nxt, r)
                    else:
                        load_in(nxt - UNITS, r + 1)
            r = ROUNDS - 1
            for unit in range(UNITS):
                sp.wait_ge(w_lo_ready, r * HALVES + 2 * unit + 2)
                nxt = unit + RAW_SLOTS
                if nxt < UNITS:
                    load_in(nxt, r)
                else:
                    load_out(nxt - UNITS, 0)
            for j in range(C_UNITS):
                sp.wait_ge(w_lo_ready, IN_HALVES + 2 * j + 2)
                nxt = j + RAW_SLOTS
                load_out(nxt % C_UNITS, nxt // C_UNITS)
                if j % 2 == 1:
                    c = j // 2
                    sp.wait_ge(m_lo_ready, ST * (c + 1))
                    sp.dma_start(x_rows_of(mixed, c, ST, SEQ), x_tiles[:, :, c * NC:(c + 1) * NC]
                                 ).then_inc(res_in[c], 16)
            with sp.Fori(1, CHUNKS - 1) as c:
                for j in range(C_UNITS):
                    sp.wait_ge(w_lo_ready, c * C_HALVES + IN_HALVES + 2 * j + 2)
                    nxt = j + RAW_SLOTS
                    if nxt < C_UNITS:
                        load_out(nxt, c)
                    else:
                        load_out(nxt - C_UNITS, c + 1)
                    if j == 3:
                        sp.wait_ge(out_added, c * ST + CREDIT)
                        sp.dma_start(out_tiles[:, :, bass.ds((c - 1) * NC, NC)],
                                     mixed[:, bass.ds((c - 1) * (ST * SEQ), ST * SEQ)].rearrange(
                                         "p (t n) -> p t n", t=ST)).then_inc(out_stored, 16)
            c = CHUNKS - 1
            for j in range(C_UNITS - RAW_SLOTS):
                sp.wait_ge(w_lo_ready, c * C_HALVES + IN_HALVES + 2 * j + 2)
                load_out(j + RAW_SLOTS, c)
            sp.wait_ge(out_added, c * ST + CREDIT)
            sp.dma_start(out_tiles[:, :, (c - 1) * NC:c * NC],
                         x_rows_of(mixed, c - 1, ST, SEQ)).then_inc(out_stored, 16)
            for t in range(ST):
                sp.wait_ge(out_added, c * ST + CREDIT + t + 1)
                sp.dma_start(out_tiles[:, t, c * NC:(c + 1) * NC],
                             x_rows_of(mixed, c, ST, SEQ)[:, t, :]).then_inc(out_stored, 16)
            sp.wait_ge(out_stored, 16 * (CHUNKS - 1 + ST))

        @block.tensor
        def _(pe):
            for t in range(ST):
                pe.wait_ge(x_normed, t + 1)
                if t == 0:
                    pe.wait_ge(const_in, CONSTS * 16)
                for b in range(2):
                    if t >= 2:
                        pe.wait_ge(h_lo_ready, 2 * (t - 2) + b + 1)
                    bank = 4 * (t % 2) + 2 * b
                    for i in range(8):
                        last = nc.tensor.transpose(ps[:, bank + i // 4, (i % 4) * P:(i % 4 + 1) * P],
                                                   x_rows[:, t, (8 * b + i) * P:(8 * b + i + 1) * P],
                                                   ident[:, :])
                    last.then_inc(x_transposed, 1)
            pe.wait_ge(h_lo_ready, 2 * ST)

            def products(dst, pairs, first, final):
                for i, (lhs, rhs) in enumerate(pairs):
                    last = nc.tensor.matmul(dst, lhs, rhs, start=first and i == 0,
                                            stop=final and i == len(pairs) - 1, skip_group_check=True)
                return last

            with pe.Fori(0, ROUNDS) as r:
                for m in range(HALVES):
                    g, hk = divmod(m, G_HALVES)
                    if hk == 0 and g == K:
                        pe.wait_ge(evacuated, r * 4 + START)
                    if hk == 0 and g == V:
                        pe.wait_ge(qk_normed, r * 2 + 1)
                    if hk == 0 and g == GA:
                        pe.wait_ge(qk_normed, r * 2 + 2)
                    if hk == 0 and g == U:
                        pe.wait_ge(evacuated, r * 4 + 1 + START)
                    if hk == 0 and g == GP:
                        pe.wait_ge(evacuated, r * 4 + 2 + START)
                    bank = 2 * (g % 2)
                    slot = m % W_SLOTS
                    pe.wait_ge(w_hi_ready, r * HALVES + m + 1)
                    for kk in range(2):
                        k = 2 * hk + kk
                        for c in range(2):
                            wcol = slice(kk * GC + c * P, kk * GC + (c + 1) * P)
                            products(ps[:, bank + c, :],
                                     [(w_hi[:, slot, wcol], h_hi[:, k, :]), (w_hi[:, slot, wcol], h_lo[:, k, :])],
                                     k == 0, False)
                    pe.wait_ge(w_lo_ready, r * HALVES + m + 1)
                    for kk in range(2):
                        k = 2 * hk + kk
                        for c in range(2):
                            wcol = slice(kk * GC + c * P, kk * GC + (c + 1) * P)
                            last = products(ps[:, bank + c, :], [(w_lo[:, slot, wcol], h_hi[:, k, :])],
                                            False, k == KT - 1)
                    last.then_inc(w_used, 1)

                    if m in (9, 17):
                        n = (m - 9) // 8
                        pe.wait_ge(squares_ready, r * 4 + n + 1)
                        if n == 0:
                            pe.wait_ge(pool_mixed, r * 2 + START)
                        else:
                            pe.wait_ge(rstd_ready, r * 4 + 1 + START)
                        for c in range(2):
                            last = nc.tensor.matmul(ps[:, S0 + c, :], ones_pair[:, :], wk(0)[:, c, :],
                                                    start=True, stop=True)
                        last.then_inc(squares_summed, 1)
                    if m == 25:
                        pe.wait_ge(evacuated, r * 4 + 1 + START)
                        pe.wait_ge(rstd_ready, r * 4 + START)
                        pe.wait_ge(head_normed, r * 2 + START)
                        for h in range(2):
                            for t in range(ST):
                                last = nc.tensor.transpose(ps[:, TB + h, t * P:(t + 1) * P],
                                                           wk(4)[:, h, t * P:(t + 1) * P], ident[:, :])
                            last.then_inc(v_transposed, 1)
                    i, odd = divmod(m - 23, 2)
                    if 0 <= i < ITEMS and not odd:
                        h, t = divmod(i, ST)
                        if i == 0:
                            pe.wait_ge(qk_lo_ready, r * 2 + 2)
                            pe.wait_ge(rstd_ready, r * 4 + 2 + START)
                        else:
                            pe.wait_ge(exp_done, r * (2 * ITEMS) + 2 * i)
                        for c in range(2):
                            rows, cols = slice(64 * c, 64 * c + 64), slice(t * P, (t + 1) * P)
                            last = products(ps[:, S0 + c, :],
                                            [(q_hi[rows, h, cols], k_hi[rows, h, :]),
                                             (q_lo[rows, h, cols], k_hi[rows, h, :]),
                                             (q_hi[rows, h, cols], k_lo[rows, h, :])], True, True)
                        last.then_inc(scored, 1)
                    i, odd = divmod(m - 26, 2)
                    if 0 <= i < ITEMS and not odd:
                        pe.wait_ge(attn_ready, r * ITEMS + i + 1)
                        if i == 0:
                            pe.wait_ge(v_lo_ready, r * 2 + 1)
                        else:
                            pe.wait_ge(at_lo_ready, r * ITEMS + i)
                        for t in range(ST):
                            last = nc.tensor.transpose(ps[:, TB, t * P:(t + 1) * P],
                                                       probs[:, 0, t * P:(t + 1) * P], ident[:, :])
                        last.then_inc(at_transposed, 1)
                    if m in (34, 43):
                        h = int(m == 43)
                        pe.wait_ge(at_lo_ready, r * ITEMS + ST * (h + 1))
                        if h == 0:
                            pe.wait_ge(v_lo_ready, r * 2 + 2)
                        else:
                            pe.wait_ge(head_normed, r * 2 + 1 + START)
                        for t in range(ST):
                            cols = slice(t * P, (t + 1) * P)
                            last = products(ps[:, OB, :],
                                            [(v_hi[:, h, cols], at_hi[:, t, :]), (v_hi[:, h, cols], at_lo[:, t, :]),
                                             (v_lo[:, h, cols], at_hi[:, t, :])], t == 0, t == ST - 1)
                        last.then_inc(head_done, 1)
                    if m in (40, 45):
                        h = int(m == 45)
                        pe.wait_ge(squares_ready, r * 4 + 3 + h)
                        if h == 0:
                            pe.wait_ge(exp_done, r * (2 * ITEMS) + 2 * ITEMS)
                        nc.tensor.matmul(ps[:, TB if h else S0, :], ones_all[:, :], head_out[:, :],
                                         start=True, stop=True).then_inc(squares_summed, 1)
                    if m == 47:
                        pe.wait_ge(diff_lo_ready, r + 1 + START)
                        pe.wait_ge(wp_lo_ready, r + 1 + START)
                        pe.wait_ge(rstd_ready, r * 4 + 3 + START)
                        for c in range(2):
                            for k in range(2):
                                wcol = slice(k * GC + c * P, k * GC + (c + 1) * P)
                                last = products(ps[:, S0 + c, :],
                                                [(k_hi[:, :, :].rearrange("p c n -> p (c n)")[:, wcol], q_hi[:, k, :]),
                                                 (k_hi[:, :, :].rearrange("p c n -> p (c n)")[:, wcol], q_lo[:, k, :]),
                                                 (k_lo[:, :, :].rearrange("p c n -> p (c n)")[:, wcol], q_hi[:, k, :])],
                                                k == 0, k == 1)
                        last.then_inc(pool_done, 1)

            pe.wait_ge(evacuated, ROUNDS * 4 + START)
            pe.wait_ge(pool_mixed, ROUNDS * 2 + START)
            pe.wait_ge(head_mixed, ROUNDS * 2 + START)
            with pe.Fori(0, CHUNKS // 2) as two:
                for j in range(2 * C_HALVES):
                    b, k = divmod(j, C_HALVES)
                    slot = j % W_SLOTS
                    if k == 0:
                        pe.wait_ge(out_added, two * (2 * ST) + b * ST + START)
                    if b == 0:
                        pe.wait_ge(m_lo_ready, k + 1)
                    pe.wait_ge(w_hi_ready, two * (2 * C_HALVES) + IN_HALVES + j + 1)
                    pe.wait_ge(w_lo_ready, two * (2 * C_HALVES) + IN_HALVES + j + 1)
                    for t in range(ST):
                        cols = slice(t * P, (t + 1) * P)
                        last = products(ps[:, ST * b + t, :],
                                        [(h_hi[:, k, cols], w_hi[:, slot, :]), (h_lo[:, k, cols], w_hi[:, slot, :]),
                                         (h_hi[:, k, cols], w_lo[:, slot, :])], k == 0, k == KT - 1)
                        if k == KT - 1 and t < ST - 1:
                            last.then_inc(out_tile_done, 1)
                    last.then_inc(w_used, 1)

        @block.scalar
        def _(act):
            for dst, src in ((ident[:, :], identity), (ones_pair[:, :], pair_ones), (cos_t[:, :], rope_cos),
                             (sin_t[:, :], rope_sin), (sw[:, :], subln_w),
                             (qw[0:64, :], q_norm_w), (qw[64:128, :], q_norm_w),
                             (kw[0:64, :], k_norm_w), (kw[64:128, :], k_norm_w)):
                act.dma_start(dst, src).then_inc(const_in, 16)
            for n, src in enumerate((lq1, lq2, lk1, lk2)):
                act.dma_start(lam_in[:, n, :], src.to_broadcast([P, HEAD_DIM])).then_inc(lam_loaded, 16)

            for started in (evacuated, rstd_ready):
                act.sem_inc(started, START)
            act.wait_ge(setup_step, 1)
            def x_high(t):
                for b in range(2):
                    act.wait_ge(x_transposed, 2 * t + b + 1)
                    bank = 4 * (t % 2) + 2 * b
                    nc.scalar.copy(h_hi[:, 8 * b:8 * b + 8, t * P:(t + 1) * P],
                                   ps[:, bank:bank + 2, :].rearrange("p b (k s) -> p (b k) s", s=P)
                                   ).then_inc(h_hi_ready, 1)

            for t in range(ST):
                act.wait_ge(x_in[t], 16)
                nc.scalar.activation(at_hi[:, :, :].rearrange("p t n -> p (t n)"), x_rows[:, t, :], ACT.Square,
                                     accum_out=x_ss[:, t:t + 1]).then_inc(x_squared, 1)
                act.wait_ge(x_squared, t + 1)
                nc.scalar.activation(x_rms[:, t:t + 1], x_ss[:, t:t + 1], ACT.Sqrt, bias=eps_t[:, :],
                                     scale=1.0 / D).then_inc(x_rms_ready, 1)
                if t >= 1:
                    x_high(t - 1)
            x_high(ST - 1)

            def split_high(h, rnd, base=0, rounds=HALVES):
                unit, part = divmod(h, 2)
                if part == 0:
                    act.wait_ge(raw_in[unit % RAW_SLOTS],
                                (rnd * (rounds // 2 // RAW_SLOTS) + (base // 2 + unit) // RAW_SLOTS + 1) * 16)
                if h >= W_SLOTS or base:
                    act.wait_ge(w_used, rnd * rounds + base + h - W_SLOTS + 1)
                nc.scalar.copy(w_hi[:, h % W_SLOTS, :], raw[:, unit % RAW_SLOTS, part * 512:part * 512 + 512]
                               ).then_inc(w_hi_ready, 1)

            for h in range(W_SLOTS):
                split_high(h, 0)
            act.wait_ge(lam_summed, 1)
            nc.scalar.activation(lam_exp[:, :], lam_sum[:, :], ACT.Exp).then_inc(lam_exped, 1)

            def rstd(dst, src, width, count, steps):
                act.wait_ge(squares_summed, count)
                nc.scalar.activation(dst, src, ACT.Ln, bias=eps_t[:, :], scale=1.0 / width).then_inc(log_ready, 1)
                act.wait_ge(log_ready, count)
                nc.scalar.activation(dst, dst, ACT.Exp, scale=-0.5).then_inc(rstd_ready, 1)

            with act.Fori(0, ROUNDS) as r:
                for m in range(1, HALVES + 1):
                    split_high(m + 3, r)
                    if m == 4:
                        act.wait_ge(wp_lo_ready, r + START)
                        act.wait_ge(pool_mixed, r * 2 + START)
                        act.dma_start(wp_raw[:, :].rearrange("p (k n) -> p k n", k=2),
                                      w_pool[:, bass.ds(r * 2, 2), :]).then_inc(wp_in, 16)
                        act.dma_start(inv_cnt[:, :], inv_count[bass.ds(r, 1), :].to_broadcast([P, SEQ])
                                      ).then_inc(inv_in, 16)
                        act.dma_start(p_scale[:, :], pool_scale[:, bass.ds(r * 2, 2)]).then_inc(scale_in, 16)
                    if m in (8, 16):
                        n = m // 8 - 1
                        act.wait_ge(w_used, r * HALVES + m)
                        if n == 0:
                            act.wait_ge(pool_mixed, r * 2 + START)
                        else:
                            act.wait_ge(qk_lo_ready, r * 2 + 1)
                        nc.scalar.activation(wk(0), ps[:, 2 * n:2 * n + 2, :], ACT.Square
                                             ).then_inc(squares_ready, 1)
                    if m in (10, 18):
                        rstd(wk(0), ps[:, S0:S0 + 2, :], HEAD_DIM, r * 4 + (m - 2) // 8, r)
                    if m in (14, 22):
                        n = (m - 14) // 8
                        act.wait_ge(qk_rotated, r * 2 + n + 1)
                        nc.scalar.copy((q_hi, k_hi)[n][:, :, :], wk(0)).then_inc(qk_hi_ready, 1)
                    if m == 24:
                        act.wait_ge(w_used, r * HALVES + 24)
                        act.wait_ge(diff_lo_ready, r + START)
                        nc.scalar.copy(wk(4), ps[:, 0:2, :]).then_inc(evacuated, 1)
                    if m == 26:
                        for h in range(2):
                            act.wait_ge(v_transposed, r * 2 + h + 1)
                            nc.scalar.copy(v_hi[:, h, :], ps[:, TB + h, :]).then_inc(v_hi_ready, 1)
                    if m == 32:
                        act.wait_ge(w_used, r * HALVES + 32)
                        act.wait_ge(head_mixed, r * 2 + START)
                        nc.scalar.activation(gate[:, :, :], ps[:, 2:4, :], ACT.Silu).then_inc(evacuated, 1)
                    i, odd = divmod(m - 25, 2)
                    if 0 <= i <= ITEMS and not odd:
                        if i >= 1:
                            act.wait_ge(at_transposed, r * ITEMS + i)
                            if i - 1 == ST:
                                act.wait_ge(head_done, r * 2 + 1)
                            t = (i - 1) % ST
                            nc.scalar.copy(at_hi[:, :, t * P:(t + 1) * P],
                                           ps[:, TB, :].rearrange("p (t s) -> p t s", t=ST)
                                           ).then_inc(at_hi_ready, 1)
                        if i < ITEMS:
                            act.wait_ge(max_ready, r * ITEMS + i + 1)
                            for c in range(2):
                                nc.scalar.activation(probs[:, c, :], ps[:, S0 + c, :], ACT.Exp,
                                                     bias=neg_max[:, c:c + 1], scale=SCALE,
                                                     accum_out=row_sum[:, c:c + 1]).then_inc(exp_done, 1)
                    if m in (36, 44):
                        h = int(m == 44)
                        act.wait_ge(head_done, r * 2 + h + 1)
                        act.wait_ge(head_mixed, r * 2 + h + START)
                        nc.scalar.activation(head_out[:, :], ps[:, OB, :], ACT.Square).then_inc(squares_ready, 1)
                    if m == 39:
                        act.wait_ge(wp_in, r * 16 + 16)
                        act.wait_ge(scored, r * ITEMS + ITEMS)
                        nc.scalar.copy(k_hi[:, 0, :], wp_raw[:, :]).then_inc(wp_hi_ready, 1)
                    if m == 40:
                        act.wait_ge(w_used, r * HALVES + 40)
                        act.wait_ge(qk_lo_ready, r * 2 + 2)
                        nc.scalar.copy(wk(0), ps[:, 0:2, :]).then_inc(evacuated, 1)
                    if m == 41:
                        rstd(head_out[:, :], ps[:, S0, :], 2 * HEAD_DIM, r * 4 + 3, r)
                    if m == 46:
                        act.wait_ge(diff_ready, r + 1)
                        nc.scalar.copy(q_hi[:, :, :], wk(4)).then_inc(diff_hi_ready, 1)
                        rstd(head_out[:, :], ps[:, TB, :], 2 * HEAD_DIM, r * 4 + 4, r)
                    if m == 48:
                        act.wait_ge(w_used, r * HALVES + HALVES)
                        nc.scalar.activation(wk(0), ps[:, 2:4, :], ACT.Silu).then_inc(evacuated, 1)

            act.wait_ge(w_used, IN_HALVES)

            def mixed_high(k):
                if k < 8:
                    act.wait_ge(head_mixed, k + 1 + START)
                else:
                    act.wait_ge(pool_mixed, k - 7 + START)
                nc.scalar.copy(h_hi[:, k, :], mixed[:, k * SEQ:(k + 1) * SEQ]).then_inc(m_hi_ready, 1)

            for k in range(KT):
                mixed_high(k)
                if k >= W_SLOTS - 1:
                    split_high(k + 1, 0, IN_HALVES)
            for h in range(KT + 1, CHUNKS * C_HALVES):
                split_high(h, 0, IN_HALVES)

        @block.vector
        def _(dve):
            steps = [0]

            def setup(ins):
                steps[0] += 1
                ins.then_inc(setup_step, 1)
                dve.wait_ge(setup_step, steps[0])

            setup(nc.vector.memset(eps_t[:, :], EPS))
            nc.vector.memset(ones_all[:, :], 1.0)
            dve.sem_inc(out_added, CREDIT)
            for started in (head_normed, head_mixed, pool_mixed, wp_lo_ready, diff_lo_ready):
                dve.sem_inc(started, START)
            dve.wait_ge(lam_loaded, 64)
            setup(nc.vector.tensor_tensor(lam_prod[:, :, :], lam_in[:, 0:2, :], lam_in[:, 2:4, :], ALU.mult))
            nc.vector.reduce_sum(lam_sum[:, :], lam_prod[:, :, :], AX_X).then_inc(lam_summed, 1)
            dve.wait_ge(const_in, CONSTS * 16)
            setup(nc.vector.tensor_scalar(sw[:, :], sw[:, :], 1.0 - LAMBDA_INIT, None, ALU.mult))

            def x_low(t):
                for b in range(2):
                    dve.wait_ge(h_hi_ready, 2 * t + b + 1)
                    bank = 4 * (t % 2) + 2 * b
                    nc.vector.tensor_tensor(h_lo[:, 8 * b:8 * b + 8, t * P:(t + 1) * P],
                                            ps[:, bank:bank + 2, :].rearrange("p b (k s) -> p (b k) s", s=P),
                                            h_hi[:, 8 * b:8 * b + 8, t * P:(t + 1) * P].bitcast(F32), ALU.subtract
                                            ).then_inc(h_lo_ready, 1)

            dve.wait_ge(norm_row_in, 16)
            for t in range(ST):
                dve.wait_ge(x_rms_ready, t + 1)
                setup(nc.vector.reciprocal(x_rstd[:, t:t + 1], x_rms[:, t:t + 1]))
                nc.vector.scalar_tensor_tensor(out=x_rows[:, t, :], in0=x_rows[:, t, :], scalar=x_rstd[:, t:t + 1],
                                               in1=norm_row, op0=ALU.mult, op1=ALU.mult).then_inc(x_normed, 1)
                if t >= 1:
                    x_low(t - 1)
            dve.wait_ge(x_normed, ST)
            setup(nc.vector.memset(wk_cols(0, 0, PAD), 0.0))
            setup(nc.vector.memset(wk_cols(0, PAD + SEQ, XW), 0.0))
            x_low(ST - 1)

            def split_low(h, rnd, base=0, rounds=HALVES):
                unit, part = divmod(h, 2)
                dve.wait_ge(w_hi_ready, rnd * rounds + base + h + 1)
                nc.vector.tensor_tensor(w_lo[:, h % W_SLOTS, :],
                                        raw[:, unit % RAW_SLOTS, part * 512:part * 512 + 512],
                                        w_hi[:, h % W_SLOTS, :].bitcast(F32), ALU.subtract).then_inc(w_lo_ready, 1)

            for h in range(W_SLOTS):
                split_low(h, 0)
            dve.wait_ge(lam_exped, 1)
            setup(nc.vector.tensor_tensor(neg_lam[:, :], lam_exp[:, 1:2], lam_exp[:, 0:1], ALU.subtract))
            setup(nc.vector.tensor_scalar(neg_lam[:, :], neg_lam[:, :], LAMBDA_INIT, None, ALU.subtract))

            with dve.Fori(0, ROUNDS) as r:
                step = [0]

                def chain(ins):
                    step[0] += 1
                    ins.then_inc(dve_step, 1)
                    dve.wait_ge(dve_step, r * STEPS + step[0])

                for m in range(1, HALVES + 1):
                    split_low(m + 3, r)
                    if m in (11, 19):
                        n = (m - 11) // 8
                        dve.wait_ge(rstd_ready, r * 4 + n + 1 + START)
                        nc.vector.scalar_tensor_tensor(out=wk(0), in0=ps[:, 2 * n:2 * n + 2, :],
                                                       scalar=(qw, kw)[n][:, :], in1=wk(0),
                                                       op0=ALU.mult, op1=ALU.mult).then_inc(qk_normed, 1)
                        dve.wait_ge(qk_normed, r * 2 + n + 1)
                        nc.vector.tensor_tensor(wk(2), wk(0), twice(cos_t), ALU.mult)
                        chain(nc.vector.stream_shuffle(wk(1), wk(0), ROPE_PARTNER))
                    if m in (12, 20):
                        chain(nc.vector.tensor_tensor(wk(1), wk(1), twice(sin_t), ALU.mult))
                    if m in (13, 21):
                        nc.vector.tensor_tensor(wk(0), wk(2), wk(1), ALU.add).then_inc(qk_rotated, 1)
                    if m in (15, 22):
                        n = int(m == 22)
                        dve.wait_ge(qk_hi_ready, r * 2 + n + 1)
                        nc.vector.tensor_tensor((q_lo, k_lo)[n][:, :, :], wk(0),
                                                (q_hi, k_hi)[n][:, :, :].bitcast(F32), ALU.subtract
                                                ).then_inc(qk_lo_ready, 1)
                    i, odd = divmod(m - 24, 2)
                    if 0 <= i <= ITEMS and not odd:
                        if i >= 1:
                            dve.wait_ge(exp_done, r * (2 * ITEMS) + 2 * i)
                            chain(nc.vector.reciprocal(row_inv[:, :], row_sum[:, :]))
                            nc.vector.tensor_tensor(coef[:, :], row_inv[:, 1:2], neg_lam[:, :], ALU.mult)
                            chain(nc.vector.tensor_scalar(probs[:, 0, :], probs[:, 0, :], row_inv[:, 0:1], None,
                                                          ALU.mult))
                            nc.vector.scalar_tensor_tensor(out=probs[:, 0, :], in0=probs[:, 1, :],
                                                           scalar=coef[:, :], in1=probs[:, 0, :],
                                                           op0=ALU.mult, op1=ALU.add).then_inc(attn_ready, 1)
                        if i < ITEMS:
                            dve.wait_ge(scored, r * ITEMS + i + 1)
                            chain(nc.vector.reduce_max(row_max[:, :], ps[:, S0:S0 + 2, :], AX_X))
                            nc.vector.tensor_scalar(neg_max[:, :], row_max[:, :], -SCALE, None, ALU.mult
                                                    ).then_inc(max_ready, 1)
                    if odd and 1 <= i <= ITEMS:
                        dve.wait_ge(at_hi_ready, r * ITEMS + i)
                        t = (i - 1) % ST
                        nc.vector.tensor_tensor(at_lo[:, :, t * P:(t + 1) * P],
                                                ps[:, TB, :].rearrange("p (t s) -> p t s", t=ST),
                                                at_hi[:, :, t * P:(t + 1) * P].bitcast(F32), ALU.subtract
                                                ).then_inc(at_lo_ready, 1)
                    if m == 26:
                        for h in range(2):
                            dve.wait_ge(v_hi_ready, r * 2 + h + 1)
                            nc.vector.tensor_tensor(v_lo[:, h, :], ps[:, TB + h, :], v_hi[:, h, :].bitcast(F32),
                                                    ALU.subtract).then_inc(v_lo_ready, 1)
                    if m == 40:
                        dve.wait_ge(wp_hi_ready, r + 1)
                        nc.vector.tensor_tensor(k_lo[:, 0, :], wp_raw[:, :], k_hi[:, 0, :].bitcast(F32),
                                                ALU.subtract).then_inc(wp_lo_ready, 1)
                    if m == 41:
                        dve.wait_ge(evacuated, r * 4 + 3 + START)
                        chain(nc.vector.tensor_tensor(wk_cols(1, 1, 527), wk_cols(0, 0, 526), wk_cols(0, 1, 527),
                                                      ALU.add))
                    if m in (42, 47):
                        h = int(m == 47)
                        dve.wait_ge(rstd_ready, r * 4 + 3 + h + START)
                        nc.vector.scalar_tensor_tensor(out=head_out[:, :], in0=ps[:, OB, :], scalar=sw[:, :],
                                                       in1=head_out[:, :], op0=ALU.mult, op1=ALU.mult
                                                       ).then_inc(head_normed, 1)
                        dve.wait_ge(head_normed, r * 2 + h + 1 + START)
                        nc.vector.tensor_tensor(mixed[:, bass.ds(r * (2 * SEQ) + h * SEQ, SEQ)], head_out[:, :],
                                                gate[:, h, :], ALU.mult).then_inc(head_mixed, 1)
                    if m == 43:
                        chain(nc.vector.tensor_tensor(wk_cols(2, 2, 526), wk_cols(1, 1, 525), wk_cols(1, 3, 527),
                                                      ALU.add))
                        chain(nc.vector.tensor_tensor(wk_cols(3, 4, 524), wk_cols(2, 2, 522), wk_cols(2, 6, 526),
                                                      ALU.add))
                    if m == 44:
                        chain(nc.vector.tensor_tensor(wk(4), wk_cols(3, 4, 516), wk_cols(3, 12, 524), ALU.add))
                    if m == 45:
                        dve.wait_ge(inv_in, r * 16 + 16)
                        chosen = work[:, bass.ds(r * (2 * XW) + 2 * XW, 2 * XW)].rearrange(
                            "p (c n) -> p c n", c=2)[:, :, PAD:PAD + SEQ]
                        chain(nc.vector.tensor_tensor(wk(4), chosen, twice(inv_cnt), ALU.mult))
                        nc.vector.tensor_tensor(wk(4), wk(4), wk(0), ALU.subtract).then_inc(diff_ready, 1)
                    if m == 46:
                        dve.wait_ge(diff_hi_ready, r + 1)
                        nc.vector.tensor_tensor(q_lo[:, :, :], wk(4), q_hi[:, :, :].bitcast(F32), ALU.subtract
                                                ).then_inc(diff_lo_ready, 1)
                    if m == 48:
                        dve.wait_ge(pool_done, r + 1)
                        dve.wait_ge(scale_in, r * 16 + 16)
                        dve.wait_ge(evacuated, r * 4 + 4 + START)
                        for c in range(2):
                            nc.vector.scalar_tensor_tensor(
                                out=mixed[:, bass.ds(r * (2 * SEQ) + (8 + c) * SEQ, SEQ)], in0=ps[:, S0 + c, :],
                                scalar=p_scale[:, c:c + 1], in1=wk(0)[:, c, :], op0=ALU.mult, op1=ALU.mult
                            ).then_inc(pool_mixed, 1)
                assert step[0] == STEPS, step[0]

            def mixed_low(k):
                dve.wait_ge(m_hi_ready, k + 1)
                nc.vector.tensor_tensor(h_lo[:, k, :], mixed[:, k * SEQ:(k + 1) * SEQ],
                                        h_hi[:, k, :].bitcast(F32), ALU.subtract).then_inc(m_lo_ready, 1)

            def add_x(chunk):
                dve.wait_ge(res_in[chunk], 16)
                for t in range(ST):
                    if t < ST - 1:
                        dve.wait_ge(out_tile_done, (ST - 1) * chunk + t + 1)
                    else:
                        dve.wait_ge(w_used, IN_HALVES + C_HALVES * (chunk + 1))
                    tile = mixed[:, (ST * chunk + t) * SEQ:(ST * chunk + t + 1) * SEQ]
                    nc.vector.tensor_tensor(tile, ps[:, 4 * (chunk % 2) + t, :], tile, ALU.add
                                            ).then_inc(out_added, 1)

            for k in range(KT):
                mixed_low(k)
                if k >= W_SLOTS - 1:
                    split_low(k + 1, 0, IN_HALVES)
            for h in range(KT + 1, CHUNKS * C_HALVES):
                split_low(h, 0, IN_HALVES)
                if h % C_HALVES == 3 and h > C_HALVES:
                    add_x(h // C_HALVES - 1)
            add_x(CHUNKS - 1)


CONSTS = 9
STEPS = 33
ROPE_PARTNER = list(range(8, 16)) + list(range(0, 8)) + list(range(16, 32))


def x_rows_of(mixed, chunk, tiles, width):
    return mixed[:, chunk * tiles * width:(chunk + 1) * tiles * width].rearrange("p (t n) -> p t n", t=tiles)


def kernel(x, norm_w, w_in, q_norm_w, k_norm_w, lambda_q1, lambda_k1, lambda_q2, lambda_k2, subln_w,
           w_pool, pool_scale, w_out):
    import numpy as np
    import concourse.bacc as bacc
    from concourse.bass_utils import run_bass_kernel_spmd

    f = np.float32
    seq, d = x.shape[1], x.shape[2]
    identity = np.eye(P, dtype=f)
    pair_ones = np.kron(np.eye(2, dtype=f), np.ones((HEAD_DIM, HEAD_DIM), f))
    half = HEAD_DIM // 8
    inv_freq = (500000.0 ** (-np.arange(0, 2 * half, 2, dtype=np.float64) / (2 * half))).astype(f)
    ang = np.arange(seq, dtype=f)[None, :] * inv_freq[:, None]
    cos, sin = np.cos(ang.astype(np.float64)).astype(f), np.sin(ang.astype(np.float64)).astype(f)
    rope_cos, rope_sin = np.ones((P, seq), f), np.zeros((P, seq), f)
    for c in (0, HEAD_DIM):
        rope_cos[c:c + half], rope_cos[c + half:c + 2 * half] = cos, cos
        rope_sin[c:c + half], rope_sin[c + half:c + 2 * half] = -sin, sin
    pos = np.arange(seq)
    inv_count = np.stack([1.0 / (np.minimum(pos + w - 1 - w // 2, seq - 1) - np.maximum(pos - w // 2, 0) + 1)
                          for w in (2, 4, 8, 16)]).astype(f)
    tiled = w_pool[0].shape[1] // P
    arrays = {
        "x": x[0], "norm_w": norm_w, "w_in": w_in[0], "q_norm_w": np.reshape(q_norm_w, (-1, 1)),
        "k_norm_w": np.reshape(k_norm_w, (-1, 1)), "lq1": lambda_q1, "lk1": lambda_k1, "lq2": lambda_q2,
        "lk2": lambda_k2, "subln_w": np.reshape(subln_w, (-1, 1)),
        "w_pool": np.reshape(np.transpose(np.reshape(w_pool[0], (-1, P, w_pool.shape[3])), (1, 0, 2)),
                             (P, N_WINDOWS * tiled, w_pool.shape[3])),
        "pool_scale": np.transpose(np.reshape(pool_scale, (-1, P))), "w_out": w_out[0],
        "identity": identity, "pair_ones": pair_ones, "rope_cos": rope_cos, "rope_sin": rope_sin,
        "inv_count": inv_count,
    }
    arrays = {n: np.ascontiguousarray(a) for n, a in arrays.items()}
    nc = bacc.Bacc("TRN2", target_bir_lowering=False, num_devices=1, dynamic_dma_scratch_size=2048)
    args = [nc.dram_tensor(f"in_{n}", a.shape, mybir.dt.from_np(a.dtype), kind="ExternalInput").ap()
            for n, a in arrays.items()]
    out = nc.dram_tensor("out", (seq, d), F32, kind="ExternalOutput").ap()
    hybrid_block(nc, *args, out)
    r = run_bass_kernel_spmd(nc, [{f"in_{n}": a for n, a in arrays.items()}], core_ids=[0])
    return r.results[0]["out"].reshape(1, seq, d)
```

```python
import math
from contextlib import ExitStack

import concourse.bass as bass
from concourse import mybir

F32 = mybir.dt.float32
F32R = mybir.dt.float32r
ALU = mybir.AluOpType
ACT = mybir.ActivationFunctionType
AX_X = mybir.AxisListType.X

P = 128
HEAD_DIM = 64
N_WINDOWS = 4
EPS = 1e-6
LAMBDA_INIT = 0.2
PAD = 8
RAW_SLOTS = 4
W_SLOTS = 4


def hybrid_block(nc, x, norm_w, w_in, q_norm_w, k_norm_w, lq1, lk1, lq2, lk2, subln_w, w_pool,
                 pool_scale, w_out, identity, pair_ones, rope_cos, rope_sin, inv_count, out):
    SEQ, D = x.shape
    KT = D // P
    ST = SEQ // P
    A = w_in.shape[1] // 6
    GC = 256
    ROUNDS = A // GC
    UNITS, HALVES = 24, 48
    G_UNITS, G_HALVES = 4, 8
    IN_HALVES = ROUNDS * HALVES
    NC = 512
    CHUNKS = D // NC
    C_UNITS, C_HALVES = KT // 2, KT
    START = 1
    CREDIT = ST + START
    ITEMS = 2 * ST
    SCALE = 1.0 / math.sqrt(HEAD_DIM)
    XW = SEQ + 2 * PAD
    Q, K, V, GA, U, GP = range(6)

    with ExitStack() as ctx:
        def sb(name, shape, dt=F32):
            return ctx.enter_context(nc.sbuf_tensor(name, shape, dt))

        def sem(name):
            return ctx.enter_context(nc.semaphore(name))

        h_hi = sb("h_hi", [P, KT, SEQ], F32R)
        h_lo = sb("h_lo", [P, KT, SEQ], F32R)
        mixed = sb("mixed", [P, KT * SEQ])
        raw = sb("raw", [P, RAW_SLOTS, 1024])
        w_hi = sb("w_hi", [P, W_SLOTS, 512], F32R)
        w_lo = sb("w_lo", [P, W_SLOTS, 512], F32R)
        q_stack = sb("q_stack", [P, 2, 2, SEQ], F32R)
        kh_twice = sb("kh_twice", [P, 2, 2, SEQ], F32R)
        kl_twice = sb("kl_twice", [P, 2, 2, SEQ], F32R)
        sq_hi, sq_lo = kh_twice[:, 1], kl_twice[:, 1]
        q_low = kl_twice[:, 0]
        hsq_hi, hsq_lo = kh_twice[:, 0, 1], kl_twice[:, 0, 1]
        wp_hi, wp_lo = kh_twice[:, 0, 0], kl_twice[:, 0, 0]
        diff_hi, diff_lo = q_stack[:, 0], q_stack[:, 1]
        work = sb("work", [P, 5 * 2 * XW])
        v_hi = sb("v_hi", [P, 2, SEQ], F32R)
        v_lo = sb("v_lo", [P, 2, SEQ], F32R)
        probs = sb("probs", [P, 2, SEQ])
        at_hi = sb("at_hi", [P, ST, SEQ], F32R)
        at_lo = sb("at_lo", [P, ST, SEQ], F32R)
        head_out = sb("head_out", [P, SEQ])
        gate = sb("gate", [P, 2, SEQ])
        wp_raw = sb("wp_raw", [P, 512])
        inv_cnt = sb("inv_cnt", [P, SEQ])
        cos_t = sb("cos_t", [P, SEQ])
        sin_t = sb("sin_t", [P, SEQ])
        ident = sb("ident", [P, P])
        ones_pair = sb("ones_pair", [P, P])
        ones_pair_r = sb("ones_pair_r", [P, P], F32R)
        ones_all_r = sb("ones_all_r", [P, P], F32R)
        qw = sb("qw", [P, 1])
        kw = sb("kw", [P, 1])
        sw = sb("sw", [P, 1])
        eps_t = sb("eps_t", [P, 1])
        p_scale = sb("p_scale", [P, 2])
        lam_in = sb("lam_in", [P, 4, HEAD_DIM])
        lam_prod = sb("lam_prod", [P, 2, HEAD_DIM])
        lam_sum = sb("lam_sum", [P, 2])
        lam_exp = sb("lam_exp", [P, 2])
        neg_lam = sb("neg_lam", [P, 1])
        x_ss = sb("x_ss", [P, ST])
        x_rms = sb("x_rms", [P, ST])
        x_rstd = sb("x_rstd", [P, ST])
        row_max = sb("row_max", [P, 2])
        neg_max = sb("neg_max", [P, 2])
        row_sum = sb("row_sum", [P, 2])
        row_inv = sb("row_inv", [P, 2])
        coef = sb("coef", [P, 1])

        ps = ctx.enter_context(nc.psum_tensor("ps", [P, 8, 512], F32))
        S0, TB, OB = 4, 6, 7

        OUT_BANKS = ((0, 1, TB, OB), (2, 3, S0, S0 + 1))

        x_rows = mixed[:, :].rearrange("p (t n) -> p t n", t=ST)
        norm_row = work[:, 0:D]

        def wk(i):
            return work[:, i * 2 * XW:(i + 1) * 2 * XW].rearrange("p (c n) -> p c n", c=2)[:, :, PAD:PAD + SEQ]

        def wk_cols(i, a, b):
            return work[:, i * 2 * XW:(i + 1) * 2 * XW].rearrange("p (c n) -> p c n", c=2)[:, :, a:b]

        def twice(t):
            return t[:, :].unsqueeze(1).to_broadcast([P, 2, SEQ])

        const_in = sem("const_in")
        lam_loaded = sem("lam_loaded")
        norm_row_in = sem("norm_row_in")
        x_in = [sem(f"x_in{i}") for i in range(ST)]
        ident_in, q_moved, k_moved = sem("ident_in"), sem("q_moved"), sem("k_moved")
        q_low_ready, squares_low_ready = sem("q_low_ready"), sem("squares_low_ready")
        x_squared, x_rms_ready, x_normed = sem("x_squared"), sem("x_rms_ready"), sem("x_normed")
        x_transposed, h_hi_ready, h_lo_ready = sem("x_transposed"), sem("h_hi_ready"), sem("h_lo_ready")
        setup_step, lam_summed, lam_exped = sem("setup_step"), sem("lam_summed"), sem("lam_exped")
        raw_in = [sem(f"raw_in{i}") for i in range(RAW_SLOTS)]
        w_hi_ready, w_lo_ready, w_used = sem("w_hi_ready"), sem("w_lo_ready"), sem("w_used")
        wp_in, inv_in, scale_in = sem("wp_in"), sem("inv_in"), sem("scale_in")
        squares_ready, squares_summed, log_ready, rstd_ready = (
            sem("squares_ready"), sem("squares_summed"), sem("log_ready"), sem("rstd_ready"))
        qk_normed, dve_step = sem("qk_normed"), sem("dve_step")
        qk_rotated, qk_hi_ready, k_low_ready = sem("qk_rotated"), sem("qk_hi_ready"), sem("k_low_ready")
        evacuated = sem("evacuated")
        v_transposed, v_hi_ready, v_lo_ready = sem("v_transposed"), sem("v_hi_ready"), sem("v_lo_ready")
        scored, max_ready, exp_done, attn_ready = sem("scored"), sem("max_ready"), sem("exp_done"), sem("attn_ready")
        at_transposed, at_hi_ready, at_lo_ready = sem("at_transposed"), sem("at_hi_ready"), sem("at_lo_ready")
        head_done, head_normed, head_mixed = sem("head_done"), sem("head_normed"), sem("head_mixed")
        wp_hi_ready, wp_lo_ready = sem("wp_hi_ready"), sem("wp_lo_ready")
        diff_ready, diff_hi_ready, diff_lo_ready = sem("diff_ready"), sem("diff_hi_ready"), sem("diff_lo_ready")
        pool_done, pool_mixed = sem("pool_done"), sem("pool_mixed")
        m_hi_ready, m_lo_ready = sem("m_hi_ready"), sem("m_lo_ready")
        res_in = [sem(f"res_in{i}") for i in range(CHUNKS)]
        out_tile_done, out_added, out_stored = sem("out_tile_done"), sem("out_added"), sem("out_stored")

        w_in_rows = w_in.rearrange("(k p) n -> p k n", p=P)
        w_out_rows = w_out.rearrange("(k p) n -> p k n", p=P)
        x_tiles = x.rearrange("(t p) n -> p t n", p=P)
        out_tiles = out.rearrange("(t p) n -> p t n", p=P)

        block = ctx.enter_context(nc.Block())

        @block.sync
        def _(sp):
            for t in range(ST):
                sp.dma_start(x_rows[:, t, :], x_tiles[:, t, :]).then_inc(x_in[t], 16)
                if t == 0:
                    sp.dma_start(norm_row, norm_w.to_broadcast([P, D])).then_inc(norm_row_in, 16)

            def load_in(unit, rnd):
                g, j = divmod(unit, G_UNITS)
                sp.dma_start(raw[:, unit % RAW_SLOTS, :].rearrange("p (k n) -> p k n", k=4),
                             w_in_rows[:, 4 * j:4 * j + 4, bass.ds(rnd * GC + g * A, GC)]
                             ).then_inc(raw_in[unit % RAW_SLOTS], 16)

            def load_out(j, chunk):
                sp.dma_start(raw[:, j % RAW_SLOTS, :].rearrange("p (k n) -> p k n", k=2),
                             w_out_rows[:, 2 * j:2 * j + 2, bass.ds(chunk * NC, NC)]
                             ).then_inc(raw_in[j % RAW_SLOTS], 16)

            for unit in range(RAW_SLOTS):
                load_in(unit, 0)
            for dst, src in ((ones_pair[:, :], pair_ones), (cos_t[:, :], rope_cos),
                             (sin_t[:, :], rope_sin), (sw[:, :], subln_w),
                             (qw[0:64, :], q_norm_w), (qw[64:128, :], q_norm_w),
                             (kw[0:64, :], k_norm_w), (kw[64:128, :], k_norm_w)):
                sp.dma_start(dst, src).then_inc(const_in, 16)
            for n, src in enumerate((lq1, lq2, lk1, lk2)):
                sp.dma_start(lam_in[:, n, :], src.to_broadcast([P, HEAD_DIM])).then_inc(lam_loaded, 16)

            def swap_halves(unit, rnd):
                if unit == 8:
                    sp.wait_ge(q_low_ready, rnd * 2 + 2)
                    sp.dma_start(q_stack[64:128, 0].bitcast(F32), q_low[0:64].bitcast(F32)).then_inc(q_moved, 16)
                    sp.dma_start(q_stack[0:64, 1].bitcast(F32), q_low[64:128].bitcast(F32)).then_inc(q_moved, 16)
                if unit == 11:
                    sp.wait_ge(qk_hi_ready, rnd * 4 + 4)
                    sp.dma_start(kh_twice[64:128, 0].bitcast(F32), kh_twice[0:64, 0].bitcast(F32)).then_inc(k_moved, 16)
                    sp.dma_start(kh_twice[0:64, 1].bitcast(F32), kh_twice[64:128, 1].bitcast(F32)).then_inc(k_moved, 16)
                    sp.wait_ge(k_low_ready, rnd * 2 + 2)
                    sp.dma_start(kl_twice[64:128, 0].bitcast(F32), kl_twice[0:64, 0].bitcast(F32)).then_inc(k_moved, 16)
                    sp.dma_start(kl_twice[0:64, 1].bitcast(F32), kl_twice[64:128, 1].bitcast(F32)).then_inc(k_moved, 16)

            with sp.Fori(0, ROUNDS - 1) as r:
                for unit in range(UNITS):
                    sp.wait_ge(w_lo_ready, r * HALVES + 2 * unit + 2)
                    nxt = unit + RAW_SLOTS
                    if nxt < UNITS:
                        load_in(nxt, r)
                    else:
                        load_in(nxt - UNITS, r + 1)
                    swap_halves(unit, r)
            r = ROUNDS - 1
            for unit in range(UNITS):
                sp.wait_ge(w_lo_ready, r * HALVES + 2 * unit + 2)
                nxt = unit + RAW_SLOTS
                if nxt < UNITS:
                    load_in(nxt, r)
                else:
                    load_out(nxt - UNITS, 0)
                swap_halves(unit, r)
            for j in range(C_UNITS):
                sp.wait_ge(w_lo_ready, IN_HALVES + 2 * j + 2)
                nxt = j + RAW_SLOTS
                load_out(nxt % C_UNITS, nxt // C_UNITS)
                if j % 2 == 1:
                    c = j // 2
                    sp.wait_ge(m_lo_ready, ST * (c + 1))
                    sp.dma_start(x_rows_of(mixed, c, ST, SEQ), x_tiles[:, :, c * NC:(c + 1) * NC]
                                 ).then_inc(res_in[c], 16)
            with sp.Fori(1, CHUNKS - 1) as c:
                for j in range(C_UNITS):
                    sp.wait_ge(w_lo_ready, c * C_HALVES + IN_HALVES + 2 * j + 2)
                    nxt = j + RAW_SLOTS
                    if nxt < C_UNITS:
                        load_out(nxt, c)
                    else:
                        load_out(nxt - C_UNITS, c + 1)
                    if j == 3:
                        sp.wait_ge(out_added, c * ST + CREDIT)
                        sp.dma_start(out_tiles[:, :, bass.ds((c - 1) * NC, NC)],
                                     mixed[:, bass.ds((c - 1) * (ST * SEQ), ST * SEQ)].rearrange(
                                         "p (t n) -> p t n", t=ST)).then_inc(out_stored, 16)
            c = CHUNKS - 1
            for j in range(C_UNITS - RAW_SLOTS):
                sp.wait_ge(w_lo_ready, c * C_HALVES + IN_HALVES + 2 * j + 2)
                load_out(j + RAW_SLOTS, c)
            sp.wait_ge(out_added, c * ST + CREDIT)
            sp.dma_start(out_tiles[:, :, (c - 1) * NC:c * NC],
                         x_rows_of(mixed, c - 1, ST, SEQ)).then_inc(out_stored, 16)
            for t in range(ST):
                sp.wait_ge(out_added, c * ST + CREDIT + t + 1)
                sp.dma_start(out_tiles[:, t, c * NC:(c + 1) * NC],
                             x_rows_of(mixed, c, ST, SEQ)[:, t, :]).then_inc(out_stored, 16)
            sp.wait_ge(out_stored, 16 * (CHUNKS - 1 + ST))

        @block.tensor
        def _(pe):
            for t in range(ST):
                pe.wait_ge(x_normed, t + 1)
                if t == 0:
                    pe.wait_ge(ident_in, 16)
                for b in range(2):
                    if t >= 2:
                        pe.wait_ge(h_lo_ready, 2 * (t - 2) + b + 1)
                    bank = 4 * (t % 2) + 2 * b
                    for i in range(8):
                        last = nc.tensor.transpose(ps[:, bank + i // 4, (i % 4) * P:(i % 4 + 1) * P],
                                                   x_rows[:, t, (8 * b + i) * P:(8 * b + i + 1) * P],
                                                   ident[:, :])
                    last.then_inc(x_transposed, 1)

            def products(dst, pairs, first, final):
                for i, (lhs, rhs) in enumerate(pairs):
                    last = nc.tensor.matmul(dst, lhs, rhs, start=first and i == 0,
                                            stop=final and i == len(pairs) - 1, skip_group_check=True)
                return last

            with pe.Fori(0, ROUNDS) as r:
                for m in range(HALVES):
                    g, hk = divmod(m, G_HALVES)
                    if hk == 0 and g == K:
                        pe.wait_ge(evacuated, r * 4 + START)
                    if hk == 0 and g == V:
                        pe.wait_ge(qk_normed, r * 2 + 1)
                    if hk == 0 and g == GA:
                        pe.wait_ge(qk_normed, r * 2 + 2)
                    if hk == 0 and g == U:
                        pe.wait_ge(evacuated, r * 4 + 1 + START)
                    if hk == 0 and g == GP:
                        pe.wait_ge(evacuated, r * 4 + 2 + START)
                    bank = 2 * (g % 2)
                    slot = m % W_SLOTS
                    if g == Q and hk in (0, 4):
                        pe.wait_ge(h_lo_ready, 2 * ST - (hk == 0))
                    pe.wait_ge(w_hi_ready, r * HALVES + m + 1)
                    for kk in range(2):
                        k = 2 * hk + kk
                        for c in range(2):
                            wcol = slice(kk * GC + c * P, kk * GC + (c + 1) * P)
                            products(ps[:, bank + c, :],
                                     [(w_hi[:, slot, wcol], h_hi[:, k, :]), (w_hi[:, slot, wcol], h_lo[:, k, :])],
                                     k == 0, False)
                    pe.wait_ge(w_lo_ready, r * HALVES + m + 1)
                    for kk in range(2):
                        k = 2 * hk + kk
                        for c in range(2):
                            wcol = slice(kk * GC + c * P, kk * GC + (c + 1) * P)
                            last = products(ps[:, bank + c, :], [(w_lo[:, slot, wcol], h_hi[:, k, :])],
                                            False, k == KT - 1)
                    last.then_inc(w_used, 1)

                    if m in (10, 17):
                        n = int(m == 17)
                        pe.wait_ge(squares_low_ready, r * 4 + n + 1)
                        if n == 0:
                            pe.wait_ge(pool_mixed, r * 2 + START)
                        else:
                            pe.wait_ge(rstd_ready, r * 4 + 1 + START)
                        for c in range(2):
                            last = products(ps[:, S0 + c, :], [(ones_pair_r[:, :], sq_hi[:, c, :]),
                                                               (ones_pair_r[:, :], sq_lo[:, c, :])], True, True)
                        last.then_inc(squares_summed, 1)
                    if m == 25:
                        pe.wait_ge(evacuated, r * 4 + 1 + START)
                        pe.wait_ge(rstd_ready, r * 4 + START)
                        pe.wait_ge(head_normed, r * 2 + START)
                        for h in range(2):
                            for t in range(ST):
                                last = nc.tensor.transpose(ps[:, TB + h, t * P:(t + 1) * P],
                                                           wk(4)[:, h, t * P:(t + 1) * P], ident[:, :])
                            last.then_inc(v_transposed, 1)
                    i, odd = divmod(m - 24, 2)
                    if 0 <= i < ITEMS and not odd:
                        h, t = divmod(i, ST)
                        if i == 0:
                            pe.wait_ge(q_moved, r * 32 + 32)
                            pe.wait_ge(k_moved, r * 64 + 64)
                            pe.wait_ge(rstd_ready, r * 4 + 2 + START)
                        else:
                            pe.wait_ge(exp_done, r * (2 * ITEMS) + 2 * i)
                        for c in range(2):
                            stacked = q_stack[:, c, h, t * P:(t + 1) * P]
                            last = products(ps[:, S0 + c, :], [(stacked, kh_twice[:, c, h, :]),
                                                               (stacked, kl_twice[:, c, h, :])], True, True)
                        last.then_inc(scored, 1)
                    i, odd = divmod(m - 27, 2)
                    if 0 <= i < ITEMS and not odd:
                        pe.wait_ge(attn_ready, r * ITEMS + i + 1)
                        if i == 0:
                            pe.wait_ge(v_lo_ready, r * 2 + 1)
                        else:
                            pe.wait_ge(at_lo_ready, r * ITEMS + i)
                        for t in range(ST):
                            last = nc.tensor.transpose(ps[:, TB, t * P:(t + 1) * P],
                                                       probs[:, 0, t * P:(t + 1) * P], ident[:, :])
                        last.then_inc(at_transposed, 1)
                    if m in (35, 43):
                        h = int(m == 43)
                        pe.wait_ge(at_lo_ready, r * ITEMS + ST * (h + 1))
                        if h == 0:
                            pe.wait_ge(v_lo_ready, r * 2 + 2)
                        else:
                            pe.wait_ge(head_normed, r * 2 + 1 + START)
                        for t in range(ST):
                            cols = slice(t * P, (t + 1) * P)
                            last = products(ps[:, OB, :],
                                            [(v_hi[:, h, cols], at_hi[:, t, :]), (v_hi[:, h, cols], at_lo[:, t, :]),
                                             (v_lo[:, h, cols], at_hi[:, t, :])], t == 0, t == ST - 1)
                        last.then_inc(head_done, 1)
                    if m in (41, 45):
                        h = int(m == 45)
                        pe.wait_ge(squares_low_ready, r * 4 + 3 + h)
                        if h == 0:
                            pe.wait_ge(exp_done, r * (2 * ITEMS) + 2 * ITEMS)
                        products(ps[:, TB if h else S0, :], [(ones_all_r[:, :], hsq_hi), (ones_all_r[:, :], hsq_lo)],
                                 True, True).then_inc(squares_summed, 1)
                    if m == 47:
                        pe.wait_ge(diff_lo_ready, r + 1 + START)
                        pe.wait_ge(wp_lo_ready, r + 1 + START)
                        pe.wait_ge(rstd_ready, r * 4 + 3 + START)
                        for c in range(2):
                            for k in range(2):
                                wcol = slice(k * GC + c * P, k * GC + (c + 1) * P)
                                last = products(ps[:, S0 + c, :],
                                                [(wp_hi[:, wcol], diff_hi[:, k, :]), (wp_hi[:, wcol], diff_lo[:, k, :]),
                                                 (wp_lo[:, wcol], diff_hi[:, k, :])],
                                                k == 0, k == 1)
                        last.then_inc(pool_done, 1)

            pe.wait_ge(evacuated, ROUNDS * 4 - 1 + START)
            pe.wait_ge(rstd_ready, ROUNDS * 4 + START)
            pe.wait_ge(head_normed, ROUNDS * 2 + START)
            with pe.Fori(0, CHUNKS // 2) as two:
                for j in range(2 * C_HALVES):
                    b, k = divmod(j, C_HALVES)
                    slot = j % W_SLOTS
                    if k == 0:
                        pe.wait_ge(out_added, two * (2 * ST) + b * ST + START)
                    if j == C_HALVES:
                        pe.wait_ge(evacuated, ROUNDS * 4 + START)
                        pe.wait_ge(pool_mixed, ROUNDS * 2 + START)
                    if b == 0:
                        pe.wait_ge(m_lo_ready, k + 1)
                    pe.wait_ge(w_hi_ready, two * (2 * C_HALVES) + IN_HALVES + j + 1)
                    pe.wait_ge(w_lo_ready, two * (2 * C_HALVES) + IN_HALVES + j + 1)
                    for t in range(ST):
                        cols = slice(t * P, (t + 1) * P)
                        last = products(ps[:, OUT_BANKS[b][t], :],
                                        [(h_hi[:, k, cols], w_hi[:, slot, :]), (h_lo[:, k, cols], w_hi[:, slot, :]),
                                         (h_hi[:, k, cols], w_lo[:, slot, :])], k == 0, k == KT - 1)
                        if k == KT - 1 and t < ST - 1:
                            last.then_inc(out_tile_done, 1)
                    last.then_inc(w_used, 1)

        @block.scalar
        def _(act):
            act.dma_start(ident[:, :], identity).then_inc(ident_in, 16)
            nc.scalar.preload_act_table(ACT.Sqrt)
            for started in (evacuated, rstd_ready):
                act.sem_inc(started, START)
            act.wait_ge(setup_step, 1)
            def x_high(t):
                for b in range(2):
                    act.wait_ge(x_transposed, 2 * t + b + 1)
                    bank = 4 * (t % 2) + 2 * b
                    nc.scalar.copy(h_hi[:, 8 * b:8 * b + 8, t * P:(t + 1) * P],
                                   ps[:, bank:bank + 2, :].rearrange("p b (k s) -> p (b k) s", s=P)
                                   ).then_inc(h_hi_ready, 1)

            for t in range(ST):
                act.wait_ge(x_in[t], 16)
                nc.scalar.activation(at_hi[:, :, :].rearrange("p t n -> p (t n)"), x_rows[:, t, :], ACT.Square,
                                     accum_out=x_ss[:, t:t + 1]).then_inc(x_squared, 1)
                act.wait_ge(x_squared, t + 1)
                nc.scalar.activation(x_rms[:, t:t + 1], x_ss[:, t:t + 1], ACT.Sqrt, bias=eps_t[:, :],
                                     scale=1.0 / D).then_inc(x_rms_ready, 1)
                if t >= 1:
                    x_high(t - 1)
            x_high(ST - 1)

            def split_high(h, rnd, base=0, rounds=HALVES):
                unit, part = divmod(h, 2)
                if part == 0:
                    act.wait_ge(raw_in[unit % RAW_SLOTS],
                                (rnd * (rounds // 2 // RAW_SLOTS) + (base // 2 + unit) // RAW_SLOTS + 1) * 16)
                if h >= W_SLOTS or base:
                    act.wait_ge(w_used, rnd * rounds + base + h - W_SLOTS + 1)
                nc.scalar.copy(w_hi[:, h % W_SLOTS, :], raw[:, unit % RAW_SLOTS, part * 512:part * 512 + 512]
                               ).then_inc(w_hi_ready, 1)

            for h in range(W_SLOTS):
                split_high(h, 0)
            act.wait_ge(lam_summed, 1)
            nc.scalar.activation(lam_exp[:, :], lam_sum[:, :], ACT.Exp).then_inc(lam_exped, 1)

            def rstd(dst, src, width, count):
                act.wait_ge(squares_summed, count)
                nc.scalar.activation(dst, src, ACT.Ln, bias=eps_t[:, :], scale=1.0 / width).then_inc(log_ready, 1)
                act.wait_ge(log_ready, count)
                nc.scalar.activation(dst, dst, ACT.Exp, scale=-0.5).then_inc(rstd_ready, 1)

            def squares(full, high, src):
                nc.scalar.activation(full, src, ACT.Square).then_inc(squares_ready, 1)
                nc.scalar.activation(high, src, ACT.Square).then_inc(squares_ready, 1)

            with act.Fori(0, ROUNDS) as r:
                for m in range(1, HALVES + 1):
                    split_high(m + 3, r)
                    if m == 4:
                        act.wait_ge(wp_lo_ready, r + START)
                        act.wait_ge(pool_mixed, r * 2 + START)
                        act.dma_start(wp_raw[:, :].rearrange("p (k n) -> p k n", k=2),
                                      w_pool[:, bass.ds(r * 2, 2), :]).then_inc(wp_in, 16)
                        act.dma_start(inv_cnt[:, :], inv_count[bass.ds(r, 1), :].to_broadcast([P, SEQ])
                                      ).then_inc(inv_in, 16)
                        act.dma_start(p_scale[:, :], pool_scale[:, bass.ds(r * 2, 2)]).then_inc(scale_in, 16)
                    if m in (8, 16):
                        n = m // 8 - 1
                        if n == 0:
                            nc.scalar.preload_act_table_set(LN_EXP)
                        act.wait_ge(w_used, r * HALVES + m)
                        if n == 0:
                            act.wait_ge(pool_mixed, r * 2 + START)
                        else:
                            act.wait_ge(q_low_ready, r * 2 + 2)
                        squares(wk(0), sq_hi, ps[:, 2 * n:2 * n + 2, :])
                    if m in (11, 18):
                        n = int(m == 18)
                        rstd(wk(0), ps[:, S0:S0 + 2, :], HEAD_DIM, r * 4 + n + 1)
                    if m in (14, 22):
                        n = (m - 14) // 8
                        act.wait_ge(qk_rotated, r * 2 + n + 1)
                        for c in range(2):
                            rows = slice(64 * c, 64 * c + 64)
                            nc.scalar.copy((q_stack, kh_twice)[n][rows, c], wk(0)[rows]).then_inc(qk_hi_ready, 1)
                    if m == 24:
                        act.wait_ge(w_used, r * HALVES + 24)
                        act.wait_ge(diff_lo_ready, r + START)
                        nc.scalar.copy(wk(4), ps[:, 0:2, :]).then_inc(evacuated, 1)
                    if m == 26:
                        for h in range(2):
                            act.wait_ge(v_transposed, r * 2 + h + 1)
                            nc.scalar.copy(v_hi[:, h, :], ps[:, TB + h, :]).then_inc(v_hi_ready, 1)
                    if m == 33:
                        nc.scalar.preload_act_table(ACT.Silu)
                        act.wait_ge(w_used, r * HALVES + 32)
                        act.wait_ge(head_mixed, r * 2 + START)
                        nc.scalar.activation(gate[:, :, :], ps[:, 2:4, :], ACT.Silu).then_inc(evacuated, 1)
                        nc.scalar.preload_act_table_set(LN_EXP)
                    i, odd = divmod(m - 26, 2)
                    if 0 <= i <= ITEMS and not odd:
                        if i >= 1:
                            act.wait_ge(at_transposed, r * ITEMS + i)
                            if i - 1 == ST:
                                act.wait_ge(head_done, r * 2 + 1)
                            t = (i - 1) % ST
                            nc.scalar.copy(at_hi[:, :, t * P:(t + 1) * P],
                                           ps[:, TB, :].rearrange("p (t s) -> p t s", t=ST)
                                           ).then_inc(at_hi_ready, 1)
                        if i < ITEMS:
                            act.wait_ge(max_ready, r * ITEMS + i + 1)
                            for c in range(2):
                                nc.scalar.activation(probs[:, c, :], ps[:, S0 + c, :], ACT.Exp,
                                                     bias=neg_max[:, c:c + 1], scale=SCALE,
                                                     accum_out=row_sum[:, c:c + 1]).then_inc(exp_done, 1)
                    if m in (39, 44):
                        h = int(m == 44)
                        act.wait_ge(head_done, r * 2 + h + 1)
                        act.wait_ge(head_mixed, r * 2 + h + START)
                        act.wait_ge(scored, r * ITEMS + ITEMS)
                        squares(head_out[:, :], hsq_hi, ps[:, OB, :])
                    if m == 41:
                        act.wait_ge(wp_in, r * 16 + 16)
                        nc.scalar.copy(wp_hi, wp_raw[:, :]).then_inc(wp_hi_ready, 1)
                    if m == 40:
                        act.wait_ge(w_used, r * HALVES + 40)
                        act.wait_ge(k_low_ready, r * 2 + 2)
                        nc.scalar.copy(wk(0), ps[:, 0:2, :]).then_inc(evacuated, 1)
                    if m == 42:
                        rstd(head_out[:, :], ps[:, S0, :], 2 * HEAD_DIM, r * 4 + 3)
                    if m == 46:
                        act.wait_ge(diff_ready, r + 1)
                        nc.scalar.copy(diff_hi, wk(4)).then_inc(diff_hi_ready, 1)
                        rstd(head_out[:, :], ps[:, TB, :], 2 * HEAD_DIM, r * 4 + 4)
                        nc.scalar.preload_act_table(ACT.Silu)
                    if m == 48:
                        act.wait_ge(w_used, r * HALVES + HALVES)
                        nc.scalar.activation(wk(0), ps[:, 2:4, :], ACT.Silu).then_inc(evacuated, 1)

            act.wait_ge(w_used, IN_HALVES)

            def mixed_high(k):
                if k < 8:
                    act.wait_ge(head_mixed, k + 1 + START)
                else:
                    act.wait_ge(pool_mixed, k - 7 + START)
                nc.scalar.copy(h_hi[:, k, :], mixed[:, k * SEQ:(k + 1) * SEQ]).then_inc(m_hi_ready, 1)

            for k in range(KT):
                mixed_high(k)
                if k >= W_SLOTS - 1:
                    split_high(k + 1, 0, IN_HALVES)
            for h in range(KT + 1, CHUNKS * C_HALVES):
                split_high(h, 0, IN_HALVES)

        @block.vector
        def _(dve):
            steps = [0]

            def setup(ins):
                steps[0] += 1
                ins.then_inc(setup_step, 1)
                dve.wait_ge(setup_step, steps[0])

            setup(nc.vector.memset(eps_t[:, :], EPS))
            dve.sem_inc(out_added, CREDIT)
            for started in (head_normed, head_mixed, pool_mixed, wp_lo_ready, diff_lo_ready):
                dve.sem_inc(started, START)

            def x_low(t):
                for b in range(2):
                    dve.wait_ge(h_hi_ready, 2 * t + b + 1)
                    bank = 4 * (t % 2) + 2 * b
                    nc.vector.tensor_tensor(h_lo[:, 8 * b:8 * b + 8, t * P:(t + 1) * P],
                                            ps[:, bank:bank + 2, :].rearrange("p b (k s) -> p (b k) s", s=P),
                                            h_hi[:, 8 * b:8 * b + 8, t * P:(t + 1) * P].bitcast(F32), ALU.subtract
                                            ).then_inc(h_lo_ready, 1)

            dve.wait_ge(norm_row_in, 16)
            for t in range(ST):
                dve.wait_ge(x_rms_ready, t + 1)
                setup(nc.vector.reciprocal(x_rstd[:, t:t + 1], x_rms[:, t:t + 1]))
                nc.vector.scalar_tensor_tensor(out=x_rows[:, t, :], in0=x_rows[:, t, :], scalar=x_rstd[:, t:t + 1],
                                               in1=norm_row, op0=ALU.mult, op1=ALU.mult).then_inc(x_normed, 1)
                if t >= 1:
                    x_low(t - 1)
            dve.wait_ge(x_normed, ST)
            setup(nc.vector.memset(wk_cols(0, 0, PAD), 0.0))
            setup(nc.vector.memset(wk_cols(0, PAD + SEQ, XW), 0.0))
            x_low(ST - 1)

            def split_low(h, rnd, base=0, rounds=HALVES):
                unit, part = divmod(h, 2)
                dve.wait_ge(w_hi_ready, rnd * rounds + base + h + 1)
                nc.vector.tensor_tensor(w_lo[:, h % W_SLOTS, :],
                                        raw[:, unit % RAW_SLOTS, part * 512:part * 512 + 512],
                                        w_hi[:, h % W_SLOTS, :].bitcast(F32), ALU.subtract).then_inc(w_lo_ready, 1)

            for h in range(W_SLOTS):
                split_low(h, 0)
            dve.wait_ge(lam_loaded, 64)
            setup(nc.vector.tensor_tensor(lam_prod[:, :, :], lam_in[:, 0:2, :], lam_in[:, 2:4, :], ALU.mult))
            nc.vector.reduce_sum(lam_sum[:, :], lam_prod[:, :, :], AX_X).then_inc(lam_summed, 1)
            dve.wait_ge(const_in, CONSTS * 16)
            setup(nc.vector.tensor_scalar(sw[:, :], sw[:, :], 1.0 - LAMBDA_INIT, None, ALU.mult))
            setup(nc.vector.tensor_copy(ones_pair_r[:, :], ones_pair[:, :]))
            setup(nc.vector.memset(ones_all_r[:, :].bitcast(F32), 1.0))
            dve.wait_ge(lam_exped, 1)
            setup(nc.vector.tensor_tensor(neg_lam[:, :], lam_exp[:, 1:2], lam_exp[:, 0:1], ALU.subtract))
            setup(nc.vector.tensor_scalar(neg_lam[:, :], neg_lam[:, :], LAMBDA_INIT, None, ALU.subtract))

            with dve.Fori(0, ROUNDS) as r:
                step = [0]

                def chain(ins):
                    step[0] += 1
                    ins.then_inc(dve_step, 1)
                    dve.wait_ge(dve_step, r * STEPS + step[0])

                for m in range(1, HALVES + 1):
                    split_low(m + 3, r)
                    if m in (9, 17):
                        n = (m - 9) // 8
                        dve.wait_ge(squares_ready, r * 8 + 2 * n + 2)
                        nc.vector.tensor_tensor(sq_lo, wk(0), sq_hi.bitcast(F32), ALU.subtract
                                                ).then_inc(squares_low_ready, 1)
                    if m in (40, 45):
                        h = int(m == 45)
                        dve.wait_ge(squares_ready, r * 8 + 2 * h + 6)
                        nc.vector.tensor_tensor(hsq_lo, head_out[:, :], hsq_hi.bitcast(F32), ALU.subtract
                                                ).then_inc(squares_low_ready, 1)
                    if m in (12, 19):
                        n = int(m == 19)
                        dve.wait_ge(rstd_ready, r * 4 + n + 1 + START)
                        nc.vector.scalar_tensor_tensor(out=wk(0), in0=ps[:, 2 * n:2 * n + 2, :],
                                                       scalar=(qw, kw)[n][:, :], in1=wk(0),
                                                       op0=ALU.mult, op1=ALU.mult).then_inc(qk_normed, 1)
                        dve.wait_ge(qk_normed, r * 2 + n + 1)
                        nc.vector.tensor_tensor(wk(2), wk(0), twice(cos_t), ALU.mult)
                        chain(nc.vector.stream_shuffle(wk(1), wk(0), ROPE_PARTNER))
                    if m in (13, 20):
                        chain(nc.vector.tensor_tensor(wk(1), wk(1), twice(sin_t), ALU.mult))
                    if m in (14, 21):
                        nc.vector.tensor_tensor(wk(0), wk(2), wk(1), ALU.add).then_inc(qk_rotated, 1)
                    if m in (15, 22):
                        n = int(m == 22)
                        if n == 1:
                            dve.wait_ge(q_moved, r * 32 + 32)
                        for c in range(2):
                            rows = slice(64 * c, 64 * c + 64)
                            dve.wait_ge(qk_hi_ready, r * 4 + 2 * n + c + 1)
                            nc.vector.tensor_tensor(kl_twice[rows, c] if n else q_low[rows], wk(0)[rows],
                                                    (q_stack, kh_twice)[n][rows, c].bitcast(F32), ALU.subtract
                                                    ).then_inc((q_low_ready, k_low_ready)[n], 1)
                    i, odd = divmod(m - 25, 2)
                    if 0 <= i <= ITEMS and not odd:
                        if i >= 1:
                            dve.wait_ge(exp_done, r * (2 * ITEMS) + 2 * i)
                            chain(nc.vector.reciprocal(row_inv[:, :], row_sum[:, :]))
                            nc.vector.tensor_tensor(coef[:, :], row_inv[:, 1:2], neg_lam[:, :], ALU.mult)
                            chain(nc.vector.tensor_scalar(probs[:, 0, :], probs[:, 0, :], row_inv[:, 0:1], None,
                                                          ALU.mult))
                            nc.vector.scalar_tensor_tensor(out=probs[:, 0, :], in0=probs[:, 1, :],
                                                           scalar=coef[:, :], in1=probs[:, 0, :],
                                                           op0=ALU.mult, op1=ALU.add).then_inc(attn_ready, 1)
                        if i < ITEMS:
                            dve.wait_ge(scored, r * ITEMS + i + 1)
                            chain(nc.vector.reduce_max(row_max[:, :], ps[:, S0:S0 + 2, :], AX_X))
                            nc.vector.tensor_scalar(neg_max[:, :], row_max[:, :], -SCALE, None, ALU.mult
                                                    ).then_inc(max_ready, 1)
                    if odd and 1 <= i <= ITEMS:
                        dve.wait_ge(at_hi_ready, r * ITEMS + i)
                        t = (i - 1) % ST
                        nc.vector.tensor_tensor(at_lo[:, :, t * P:(t + 1) * P],
                                                ps[:, TB, :].rearrange("p (t s) -> p t s", t=ST),
                                                at_hi[:, :, t * P:(t + 1) * P].bitcast(F32), ALU.subtract
                                                ).then_inc(at_lo_ready, 1)
                    if m == 26:
                        for h in range(2):
                            dve.wait_ge(v_hi_ready, r * 2 + h + 1)
                            nc.vector.tensor_tensor(v_lo[:, h, :], ps[:, TB + h, :], v_hi[:, h, :].bitcast(F32),
                                                    ALU.subtract).then_inc(v_lo_ready, 1)
                    if m == 42:
                        dve.wait_ge(wp_hi_ready, r + 1)
                        nc.vector.tensor_tensor(wp_lo, wp_raw[:, :], wp_hi.bitcast(F32),
                                                ALU.subtract).then_inc(wp_lo_ready, 1)
                    if m == 41:
                        dve.wait_ge(evacuated, r * 4 + 3 + START)
                        chain(nc.vector.tensor_tensor(wk_cols(1, 1, 527), wk_cols(0, 0, 526), wk_cols(0, 1, 527),
                                                      ALU.add))
                    if m in (43, 47):
                        h = int(m == 47)
                        dve.wait_ge(rstd_ready, r * 4 + 3 + h + START)
                        nc.vector.scalar_tensor_tensor(out=head_out[:, :], in0=ps[:, OB, :], scalar=sw[:, :],
                                                       in1=head_out[:, :], op0=ALU.mult, op1=ALU.mult
                                                       ).then_inc(head_normed, 1)
                        dve.wait_ge(head_normed, r * 2 + h + 1 + START)
                        nc.vector.tensor_tensor(mixed[:, bass.ds(r * (2 * SEQ) + h * SEQ, SEQ)], head_out[:, :],
                                                gate[:, h, :], ALU.mult).then_inc(head_mixed, 1)
                    if m == 43:
                        chain(nc.vector.tensor_tensor(wk_cols(2, 2, 526), wk_cols(1, 1, 525), wk_cols(1, 3, 527),
                                                      ALU.add))
                        chain(nc.vector.tensor_tensor(wk_cols(3, 4, 524), wk_cols(2, 2, 522), wk_cols(2, 6, 526),
                                                      ALU.add))
                    if m == 44:
                        chain(nc.vector.tensor_tensor(wk(4), wk_cols(3, 4, 516), wk_cols(3, 12, 524), ALU.add))
                    if m == 45:
                        dve.wait_ge(inv_in, r * 16 + 16)
                        chosen = work[:, bass.ds(r * (2 * XW) + 2 * XW, 2 * XW)].rearrange(
                            "p (c n) -> p c n", c=2)[:, :, PAD:PAD + SEQ]
                        chain(nc.vector.tensor_tensor(wk(4), chosen, twice(inv_cnt), ALU.mult))
                        nc.vector.tensor_tensor(wk(4), wk(4), wk(0), ALU.subtract).then_inc(diff_ready, 1)
                    if m == 46:
                        dve.wait_ge(diff_hi_ready, r + 1)
                        nc.vector.tensor_tensor(diff_lo, wk(4), diff_hi.bitcast(F32), ALU.subtract
                                                ).then_inc(diff_lo_ready, 1)
                    if m == 48:
                        dve.wait_ge(pool_done, r + 1)
                        dve.wait_ge(scale_in, r * 16 + 16)
                        dve.wait_ge(evacuated, r * 4 + 4 + START)
                        for c in range(2):
                            nc.vector.scalar_tensor_tensor(
                                out=mixed[:, bass.ds(r * (2 * SEQ) + (8 + c) * SEQ, SEQ)], in0=ps[:, S0 + c, :],
                                scalar=p_scale[:, c:c + 1], in1=wk(0)[:, c, :], op0=ALU.mult, op1=ALU.mult
                            ).then_inc(pool_mixed, 1)
                assert step[0] == STEPS, step[0]

            def mixed_low(k):
                dve.wait_ge(m_hi_ready, k + 1)
                nc.vector.tensor_tensor(h_lo[:, k, :], mixed[:, k * SEQ:(k + 1) * SEQ],
                                        h_hi[:, k, :].bitcast(F32), ALU.subtract).then_inc(m_lo_ready, 1)

            def add_x(chunk):
                dve.wait_ge(res_in[chunk], 16)
                for t in range(ST):
                    if t < ST - 1:
                        dve.wait_ge(out_tile_done, (ST - 1) * chunk + t + 1)
                    else:
                        dve.wait_ge(w_used, IN_HALVES + C_HALVES * (chunk + 1))
                    tile = mixed[:, (ST * chunk + t) * SEQ:(ST * chunk + t + 1) * SEQ]
                    nc.vector.tensor_tensor(tile, ps[:, OUT_BANKS[chunk % 2][t], :], tile, ALU.add
                                            ).then_inc(out_added, 1)

            for k in range(KT):
                mixed_low(k)
                if k >= W_SLOTS - 1:
                    split_low(k + 1, 0, IN_HALVES)
            for h in range(KT + 1, CHUNKS * C_HALVES):
                split_low(h, 0, IN_HALVES)
                if h % C_HALVES == 3 and h > C_HALVES:
                    add_x(h // C_HALVES - 1)
            add_x(CHUNKS - 1)


CONSTS = 8
LN_EXP = "natural_log_exp_and_others"
STEPS = 33
ROPE_PARTNER = list(range(8, 16)) + list(range(0, 8)) + list(range(16, 32))


def x_rows_of(mixed, chunk, tiles, width):
    return mixed[:, chunk * tiles * width:(chunk + 1) * tiles * width].rearrange("p (t n) -> p t n", t=tiles)


def kernel(x, norm_w, w_in, q_norm_w, k_norm_w, lambda_q1, lambda_k1, lambda_q2, lambda_k2, subln_w,
           w_pool, pool_scale, w_out):
    import numpy as np
    import concourse.bacc as bacc
    from concourse.bass_utils import run_bass_kernel_spmd

    f = np.float32
    seq, d = x.shape[1], x.shape[2]
    identity = np.eye(P, dtype=f)
    pair_ones = np.kron(np.eye(2, dtype=f), np.ones((HEAD_DIM, HEAD_DIM), f))
    half = HEAD_DIM // 8
    inv_freq = (500000.0 ** (-np.arange(0, 2 * half, 2, dtype=np.float64) / (2 * half))).astype(f)
    ang = np.arange(seq, dtype=f)[None, :] * inv_freq[:, None]
    cos, sin = np.cos(ang.astype(np.float64)).astype(f), np.sin(ang.astype(np.float64)).astype(f)
    rope_cos, rope_sin = np.ones((P, seq), f), np.zeros((P, seq), f)
    for c in (0, HEAD_DIM):
        rope_cos[c:c + half], rope_cos[c + half:c + 2 * half] = cos, cos
        rope_sin[c:c + half], rope_sin[c + half:c + 2 * half] = -sin, sin
    pos = np.arange(seq)
    inv_count = np.stack([1.0 / (np.minimum(pos + w - 1 - w // 2, seq - 1) - np.maximum(pos - w // 2, 0) + 1)
                          for w in (2, 4, 8, 16)]).astype(f)
    tiled = w_pool[0].shape[1] // P
    arrays = {
        "x": x[0], "norm_w": norm_w, "w_in": w_in[0], "q_norm_w": np.reshape(q_norm_w, (-1, 1)),
        "k_norm_w": np.reshape(k_norm_w, (-1, 1)), "lq1": lambda_q1, "lk1": lambda_k1, "lq2": lambda_q2,
        "lk2": lambda_k2, "subln_w": np.reshape(subln_w, (-1, 1)),
        "w_pool": np.reshape(np.transpose(np.reshape(w_pool[0], (-1, P, w_pool.shape[3])), (1, 0, 2)),
                             (P, N_WINDOWS * tiled, w_pool.shape[3])),
        "pool_scale": np.transpose(np.reshape(pool_scale, (-1, P))), "w_out": w_out[0],
        "identity": identity, "pair_ones": pair_ones, "rope_cos": rope_cos, "rope_sin": rope_sin,
        "inv_count": inv_count,
    }
    arrays = {n: np.ascontiguousarray(a) for n, a in arrays.items()}
    nc = bacc.Bacc("TRN2", target_bir_lowering=False, num_devices=1, dynamic_dma_scratch_size=2048)
    args = [nc.dram_tensor(f"in_{n}", a.shape, mybir.dt.from_np(a.dtype), kind="ExternalInput").ap()
            for n, a in arrays.items()]
    out = nc.dram_tensor("out", (seq, d), F32, kind="ExternalOutput").ap()
    hybrid_block(nc, *args, out)
    r = run_bass_kernel_spmd(nc, [{f"in_{n}": a for n, a in arrays.items()}], core_ids=[0])
    return r.results[0]["out"].reshape(1, seq, d)
```

```python
import math
from contextlib import ExitStack

import concourse.bass as bass
from concourse import mybir

F32 = mybir.dt.float32
F32R = mybir.dt.float32r
ALU = mybir.AluOpType
ACT = mybir.ActivationFunctionType
AX_X = mybir.AxisListType.X

P = 128
HEAD_DIM = 64
N_WINDOWS = 4
EPS = 1e-6
LAMBDA_INIT = 0.2
PAD = 8
RAW_SLOTS = 4
W_SLOTS = 4


def hybrid_block(nc, x, norm_w, w_in, q_norm_w, k_norm_w, lq1, lk1, lq2, lk2, subln_w, w_pool,
                 pool_scale, w_out, identity, pair_ones, rope_cos, rope_sin, inv_count, out):
    SEQ, D = x.shape
    KT = D // P
    ST = SEQ // P
    A = w_in.shape[1] // 6
    GC = 256
    ROUNDS = A // GC
    UNITS, HALVES = 24, 48
    G_UNITS, G_HALVES = 4, 8
    IN_HALVES = ROUNDS * HALVES
    NC = 512
    CHUNKS = D // NC
    C_UNITS, C_HALVES = KT // 2, KT
    START = 1
    CREDIT = ST + START
    ITEMS = 2 * ST
    SCALE = 1.0 / math.sqrt(HEAD_DIM)
    XW = SEQ + 2 * PAD
    K, Q, V, GA, U, GP = range(6)
    COLUMNS = (A, 0, 2 * A, 3 * A, 4 * A, 5 * A)

    with ExitStack() as ctx:
        def sb(name, shape, dt=F32):
            return ctx.enter_context(nc.sbuf_tensor(name, shape, dt))

        def sem(name):
            return ctx.enter_context(nc.semaphore(name))

        h_hi = sb("h_hi", [P, KT, SEQ], F32R)
        h_lo = sb("h_lo", [P, KT, SEQ], F32R)
        mixed = sb("mixed", [P, KT * SEQ])
        raw = sb("raw", [P, RAW_SLOTS, 1024])
        w_hi = sb("w_hi", [P, W_SLOTS, 512], F32R)
        w_lo = sb("w_lo", [P, W_SLOTS, 512], F32R)
        q_stack = sb("q_stack", [P, 2, 2, SEQ], F32R)
        kh_twice = sb("kh_twice", [P, 2, 2, SEQ], F32R)
        kl_twice = sb("kl_twice", [P, 2, 2, SEQ], F32R)
        sq_hi, sq_lo = q_stack[:, 0], q_stack[:, 1]
        hsq_hi, hsq_lo = kh_twice[:, 0, 1], kl_twice[:, 0, 1]
        wp_hi, wp_lo = kh_twice[:, 0, 0], kl_twice[:, 0, 0]
        diff_hi, diff_lo = q_stack[:, 0], q_stack[:, 1]
        work = sb("work", [P, 5 * 2 * XW])
        v_hi = sb("v_hi", [P, 2, SEQ], F32R)
        v_lo = sb("v_lo", [P, 2, SEQ], F32R)
        q_low = v_hi
        probs = sb("probs", [P, 2, SEQ])
        at_hi = sb("at_hi", [P, ST, SEQ], F32R)
        at_lo = sb("at_lo", [P, ST, SEQ], F32R)
        head_out = sb("head_out", [P, SEQ])
        gate = sb("gate", [P, 2, SEQ])
        wp_raw = sb("wp_raw", [P, 512])
        inv_cnt = sb("inv_cnt", [P, SEQ])
        cos_t = sb("cos_t", [P, SEQ])
        sin_t = sb("sin_t", [P, SEQ])
        ident = sb("ident", [P, P])
        ones_pair = sb("ones_pair", [P, P])
        ones_pair_r = sb("ones_pair_r", [P, P], F32R)
        ones_all_r = sb("ones_all_r", [P, P], F32R)
        qw = sb("qw", [P, 1])
        kw = sb("kw", [P, 1])
        sw = sb("sw", [P, 1])
        eps_t = sb("eps_t", [P, 1])
        p_scale = sb("p_scale", [P, 2])
        lam_in = sb("lam_in", [P, 4, HEAD_DIM])
        lam_prod = sb("lam_prod", [P, 2, HEAD_DIM])
        lam_sum = sb("lam_sum", [P, 2])
        lam_exp = sb("lam_exp", [P, 2])
        neg_lam = sb("neg_lam", [P, 1])
        x_ss = sb("x_ss", [P, ST])
        x_rms = sb("x_rms", [P, ST])
        x_rstd = sb("x_rstd", [P, ST])
        row_max = sb("row_max", [P, 2])
        neg_max = sb("neg_max", [P, 2])
        row_sum = sb("row_sum", [P, 2])
        row_inv = sb("row_inv", [P, 2])
        coef = sb("coef", [P, 1])

        ps = ctx.enter_context(nc.psum_tensor("ps", [P, 8, 512], F32))
        S0, TB, OB = 4, 6, 7

        OUT_BANKS = ((0, 1, TB, OB), (2, 3, S0, S0 + 1))

        x_rows = mixed[:, :].rearrange("p (t n) -> p t n", t=ST)
        norm_row = work[:, 0:D]
        norm_source = work[0:1, D:2 * D]

        def wk(i):
            return work[:, i * 2 * XW:(i + 1) * 2 * XW].rearrange("p (c n) -> p c n", c=2)[:, :, PAD:PAD + SEQ]

        def wk_cols(i, a, b):
            return work[:, i * 2 * XW:(i + 1) * 2 * XW].rearrange("p (c n) -> p c n", c=2)[:, :, a:b]

        def twice(t):
            return t[:, :].unsqueeze(1).to_broadcast([P, 2, SEQ])

        const_in = sem("const_in")
        lam_loaded = sem("lam_loaded")
        norm_row_in = sem("norm_row_in")
        x_in = [sem(f"x_in{i}") for i in range(ST)]
        norm_spread, rstd_squared = sem("norm_spread"), sem("rstd_squared")
        ident_in, q_moved, k_moved = sem("ident_in"), sem("q_moved"), sem("k_moved")
        q_low_ready, squares_low_ready = sem("q_low_ready"), sem("squares_low_ready")
        x_squared, x_rms_ready, x_normed = sem("x_squared"), sem("x_rms_ready"), sem("x_normed")
        x_transposed, h_hi_ready, h_lo_ready = sem("x_transposed"), sem("h_hi_ready"), sem("h_lo_ready")
        setup_step, lam_summed, lam_exped = sem("setup_step"), sem("lam_summed"), sem("lam_exped")
        raw_in = [sem(f"raw_in{i}") for i in range(RAW_SLOTS)]
        w_hi_ready, w_lo_ready, w_used = sem("w_hi_ready"), sem("w_lo_ready"), sem("w_used")
        wp_in, inv_in, scale_in = sem("wp_in"), sem("inv_in"), sem("scale_in")
        squares_ready, squares_summed, log_ready, rstd_ready = (
            sem("squares_ready"), sem("squares_summed"), sem("log_ready"), sem("rstd_ready"))
        qk_normed, dve_step = sem("qk_normed"), sem("dve_step")
        qk_rotated, qk_hi_ready, k_low_ready = sem("qk_rotated"), sem("qk_hi_ready"), sem("k_low_ready")
        evacuated = sem("evacuated")
        v_transposed, v_hi_ready, v_lo_ready = sem("v_transposed"), sem("v_hi_ready"), sem("v_lo_ready")
        scored, max_ready, exp_done, attn_ready = sem("scored"), sem("max_ready"), sem("exp_done"), sem("attn_ready")
        at_transposed, at_hi_ready, at_lo_ready = sem("at_transposed"), sem("at_hi_ready"), sem("at_lo_ready")
        head_done, head_normed, head_mixed = sem("head_done"), sem("head_normed"), sem("head_mixed")
        wp_hi_ready, wp_lo_ready = sem("wp_hi_ready"), sem("wp_lo_ready")
        diff_ready, diff_hi_ready, diff_lo_ready = sem("diff_ready"), sem("diff_hi_ready"), sem("diff_lo_ready")
        pool_done, pool_mixed = sem("pool_done"), sem("pool_mixed")
        m_hi_ready, m_lo_ready = sem("m_hi_ready"), sem("m_lo_ready")
        res_in = [sem(f"res_in{i}") for i in range(CHUNKS)]
        out_tile_done, out_added, out_stored = sem("out_tile_done"), sem("out_added"), sem("out_stored")

        w_in_rows = w_in.rearrange("(k p) n -> p k n", p=P)
        w_out_rows = w_out.rearrange("(k p) n -> p k n", p=P)
        x_tiles = x.rearrange("(t p) n -> p t n", p=P)
        out_tiles = out.rearrange("(t p) n -> p t n", p=P)

        block = ctx.enter_context(nc.Block())

        @block.sync
        def _(sp):
            for t in range(ST):
                sp.dma_start(x_rows[:, t, :], x_tiles[:, t, :]).then_inc(x_in[t], 16)

            def load_in(unit, rnd):
                g, j = divmod(unit, G_UNITS)
                sp.dma_start(raw[:, unit % RAW_SLOTS, :].rearrange("p (k n) -> p k n", k=4),
                             w_in_rows[:, 4 * j:4 * j + 4, bass.ds(rnd * GC + COLUMNS[g], GC)]
                             ).then_inc(raw_in[unit % RAW_SLOTS], 16)

            def load_out(j, chunk):
                sp.dma_start(raw[:, j % RAW_SLOTS, :].rearrange("p (k n) -> p k n", k=2),
                             w_out_rows[:, 2 * j:2 * j + 2, bass.ds(chunk * NC, NC)]
                             ).then_inc(raw_in[j % RAW_SLOTS], 16)

            for unit in range(RAW_SLOTS):
                load_in(unit, 0)
            for dst, src in ((ones_pair[:, :], pair_ones), (cos_t[:, :], rope_cos),
                             (sin_t[:, :], rope_sin), (sw[:, :], subln_w),
                             (qw[0:64, :], q_norm_w), (qw[64:128, :], q_norm_w),
                             (kw[0:64, :], k_norm_w), (kw[64:128, :], k_norm_w)):
                sp.dma_start(dst, src).then_inc(const_in, 16)
            for n, src in enumerate((lq1, lq2, lk1, lk2)):
                sp.dma_start(lam_in[:, n, :], src.to_broadcast([P, HEAD_DIM])).then_inc(lam_loaded, 16)

            def swap_halves(unit, rnd):
                if unit == 11:
                    sp.wait_ge(q_low_ready, rnd * 2 + 2)
                    sp.dma_start(q_stack[64:128, 0].bitcast(F32), q_low[0:64].bitcast(F32)).then_inc(q_moved, 16)
                    sp.dma_start(q_stack[0:64, 1].bitcast(F32), q_low[64:128].bitcast(F32)).then_inc(q_moved, 16)
                if unit == 10:
                    sp.wait_ge(qk_hi_ready, rnd * 4 + 2)
                    sp.dma_start(kh_twice[64:128, 0].bitcast(F32), kh_twice[0:64, 0].bitcast(F32)).then_inc(k_moved, 16)
                    sp.dma_start(kh_twice[0:64, 1].bitcast(F32), kh_twice[64:128, 1].bitcast(F32)).then_inc(k_moved, 16)
                    sp.wait_ge(k_low_ready, rnd * 2 + 2)
                    sp.dma_start(kl_twice[64:128, 0].bitcast(F32), kl_twice[0:64, 0].bitcast(F32)).then_inc(k_moved, 16)
                    sp.dma_start(kl_twice[0:64, 1].bitcast(F32), kl_twice[64:128, 1].bitcast(F32)).then_inc(k_moved, 16)

            with sp.Fori(0, ROUNDS - 1) as r:
                for unit in range(UNITS):
                    sp.wait_ge(w_lo_ready, r * HALVES + 2 * unit + 2)
                    nxt = unit + RAW_SLOTS
                    if nxt < UNITS:
                        load_in(nxt, r)
                    else:
                        load_in(nxt - UNITS, r + 1)
                    swap_halves(unit, r)
            r = ROUNDS - 1
            for unit in range(UNITS):
                sp.wait_ge(w_lo_ready, r * HALVES + 2 * unit + 2)
                nxt = unit + RAW_SLOTS
                if nxt < UNITS:
                    load_in(nxt, r)
                else:
                    load_out(nxt - UNITS, 0)
                swap_halves(unit, r)
            for j in range(C_UNITS):
                sp.wait_ge(w_lo_ready, IN_HALVES + 2 * j + 2)
                nxt = j + RAW_SLOTS
                load_out(nxt % C_UNITS, nxt // C_UNITS)
                if j % 2 == 1:
                    c = j // 2
                    sp.wait_ge(m_lo_ready, ST * (c + 1))
                    sp.dma_start(x_rows_of(mixed, c, ST, SEQ), x_tiles[:, :, c * NC:(c + 1) * NC]
                                 ).then_inc(res_in[c], 16)
            with sp.Fori(1, CHUNKS - 1) as c:
                for j in range(C_UNITS):
                    sp.wait_ge(w_lo_ready, c * C_HALVES + IN_HALVES + 2 * j + 2)
                    nxt = j + RAW_SLOTS
                    if nxt < C_UNITS:
                        load_out(nxt, c)
                    else:
                        load_out(nxt - C_UNITS, c + 1)
                    if j == 3:
                        sp.wait_ge(out_added, c * ST + CREDIT)
                        sp.dma_start(out_tiles[:, :, bass.ds((c - 1) * NC, NC)],
                                     mixed[:, bass.ds((c - 1) * (ST * SEQ), ST * SEQ)].rearrange(
                                         "p (t n) -> p t n", t=ST)).then_inc(out_stored, 16)
            c = CHUNKS - 1
            for j in range(C_UNITS - RAW_SLOTS):
                sp.wait_ge(w_lo_ready, c * C_HALVES + IN_HALVES + 2 * j + 2)
                load_out(j + RAW_SLOTS, c)
            sp.wait_ge(out_added, c * ST + CREDIT)
            sp.dma_start(out_tiles[:, :, (c - 1) * NC:c * NC],
                         x_rows_of(mixed, c - 1, ST, SEQ)).then_inc(out_stored, 16)
            for t in range(ST):
                sp.wait_ge(out_added, c * ST + CREDIT + t + 1)
                sp.dma_start(out_tiles[:, t, c * NC:(c + 1) * NC],
                             x_rows_of(mixed, c, ST, SEQ)[:, t, :]).then_inc(out_stored, 16)
            sp.wait_ge(out_stored, 16 * (CHUNKS - 1 + ST))

        @block.gpsimd
        def _(pool):
            pool.wait_ge(norm_row_in, 16)
            nc.gpsimd.partition_broadcast(norm_row, norm_source, P).then_inc(norm_spread, 1)

        @block.tensor
        def _(pe):
            for t in range(ST):
                pe.wait_ge(x_normed, t + 1)
                if t == 0:
                    pe.wait_ge(ident_in, 16)
                for b in range(2):
                    if t >= 2:
                        pe.wait_ge(h_lo_ready, 2 * (t - 2) + b + 1)
                    bank = 4 * (t % 2) + 2 * b
                    for i in range(8):
                        last = nc.tensor.transpose(ps[:, bank + i // 4, (i % 4) * P:(i % 4 + 1) * P],
                                                   x_rows[:, t, (8 * b + i) * P:(8 * b + i + 1) * P],
                                                   ident[:, :])
                    last.then_inc(x_transposed, 1)

            def products(dst, pairs, first, final):
                for i, (lhs, rhs) in enumerate(pairs):
                    last = nc.tensor.matmul(dst, lhs, rhs, start=first and i == 0,
                                            stop=final and i == len(pairs) - 1, skip_group_check=True)
                return last

            with pe.Fori(0, ROUNDS) as r:
                for m in range(HALVES):
                    g, hk = divmod(m, G_HALVES)
                    if hk == 0 and g == Q:
                        pe.wait_ge(evacuated, r * 4 + START)
                    if hk == 0 and g == V:
                        pe.wait_ge(qk_normed, r * 2 + 1)
                    if hk == 0 and g == GA:
                        pe.wait_ge(qk_normed, r * 2 + 2)
                    if hk == 0 and g == U:
                        pe.wait_ge(evacuated, r * 4 + 1 + START)
                    if hk == 0 and g == GP:
                        pe.wait_ge(evacuated, r * 4 + 2 + START)
                    bank = 2 * (g % 2)
                    slot = m % W_SLOTS
                    if g == K and hk in (0, 4):
                        pe.wait_ge(h_lo_ready, 2 * ST - (hk == 0))
                    pe.wait_ge(w_hi_ready, r * HALVES + m + 1)
                    for kk in range(2):
                        k = 2 * hk + kk
                        for c in range(2):
                            wcol = slice(kk * GC + c * P, kk * GC + (c + 1) * P)
                            products(ps[:, bank + c, :],
                                     [(w_hi[:, slot, wcol], h_hi[:, k, :]), (w_hi[:, slot, wcol], h_lo[:, k, :])],
                                     k == 0, False)
                    pe.wait_ge(w_lo_ready, r * HALVES + m + 1)
                    for kk in range(2):
                        k = 2 * hk + kk
                        for c in range(2):
                            wcol = slice(kk * GC + c * P, kk * GC + (c + 1) * P)
                            last = products(ps[:, bank + c, :], [(w_lo[:, slot, wcol], h_hi[:, k, :])],
                                            False, k == KT - 1)
                    last.then_inc(w_used, 1)

                    if m in (9, 17):
                        n = int(m == 17)
                        pe.wait_ge(squares_low_ready, r * 4 + n + 1)
                        if n == 0:
                            pe.wait_ge(pool_mixed, r * 2 + START)
                        else:
                            pe.wait_ge(qk_normed, r * 2 + 1)
                        for c in range(2):
                            last = products(ps[:, S0 + c, :], [(ones_pair_r[:, :], sq_hi[:, c, :]),
                                                               (ones_pair_r[:, :], sq_lo[:, c, :])], True, True)
                        last.then_inc(squares_summed, 1)
                    if m == 25:
                        pe.wait_ge(evacuated, r * 4 + 1 + START)
                        pe.wait_ge(rstd_ready, r * 4 + START)
                        pe.wait_ge(head_normed, r * 2 + START)
                        for h in range(2):
                            for t in range(ST):
                                last = nc.tensor.transpose(ps[:, TB + h, t * P:(t + 1) * P],
                                                           wk(4)[:, h, t * P:(t + 1) * P], ident[:, :])
                            last.then_inc(v_transposed, 1)
                    i, odd = divmod(m - 24, 2)
                    if 0 <= i < ITEMS and not odd:
                        h, t = divmod(i, ST)
                        if i == 0:
                            pe.wait_ge(q_moved, r * 32 + 32)
                            pe.wait_ge(k_moved, r * 64 + 64)
                            pe.wait_ge(rstd_ready, r * 4 + 2 + START)
                        else:
                            pe.wait_ge(exp_done, r * (2 * ITEMS) + 2 * i)
                        for c in range(2):
                            stacked = q_stack[:, c, h, t * P:(t + 1) * P]
                            last = products(ps[:, S0 + c, :], [(stacked, kh_twice[:, c, h, :]),
                                                               (stacked, kl_twice[:, c, h, :])], True, True)
                        last.then_inc(scored, 1)
                    i, odd = divmod(m - 27, 2)
                    if 0 <= i < ITEMS and not odd:
                        pe.wait_ge(attn_ready, r * ITEMS + i + 1)
                        if i == 0:
                            pe.wait_ge(v_lo_ready, r * 2 + 1)
                        else:
                            pe.wait_ge(at_lo_ready, r * ITEMS + i)
                        for t in range(ST):
                            last = nc.tensor.transpose(ps[:, TB, t * P:(t + 1) * P],
                                                       probs[:, 0, t * P:(t + 1) * P], ident[:, :])
                        last.then_inc(at_transposed, 1)
                    if m in (35, 43):
                        h = int(m == 43)
                        pe.wait_ge(at_lo_ready, r * ITEMS + ST * (h + 1))
                        if h == 0:
                            pe.wait_ge(v_lo_ready, r * 2 + 2)
                        else:
                            pe.wait_ge(head_normed, r * 2 + 1 + START)
                        for t in range(ST):
                            cols = slice(t * P, (t + 1) * P)
                            last = products(ps[:, OB, :],
                                            [(v_hi[:, h, cols], at_hi[:, t, :]), (v_hi[:, h, cols], at_lo[:, t, :]),
                                             (v_lo[:, h, cols], at_hi[:, t, :])], t == 0, t == ST - 1)
                        last.then_inc(head_done, 1)
                    if m in (41, 45):
                        h = int(m == 45)
                        pe.wait_ge(squares_low_ready, r * 4 + 3 + h)
                        if h == 0:
                            pe.wait_ge(exp_done, r * (2 * ITEMS) + 2 * ITEMS)
                        products(ps[:, TB if h else S0, :], [(ones_all_r[:, :], hsq_hi), (ones_all_r[:, :], hsq_lo)],
                                 True, True).then_inc(squares_summed, 1)
                    if m == 47:
                        pe.wait_ge(diff_lo_ready, r + 1 + START)
                        pe.wait_ge(wp_lo_ready, r + 1 + START)
                        pe.wait_ge(rstd_ready, r * 4 + 3 + START)
                        for c in range(2):
                            for k in range(2):
                                wcol = slice(k * GC + c * P, k * GC + (c + 1) * P)
                                last = products(ps[:, S0 + c, :],
                                                [(wp_hi[:, wcol], diff_hi[:, k, :]), (wp_hi[:, wcol], diff_lo[:, k, :]),
                                                 (wp_lo[:, wcol], diff_hi[:, k, :])],
                                                k == 0, k == 1)
                        last.then_inc(pool_done, 1)

            pe.wait_ge(evacuated, ROUNDS * 4 - 1 + START)
            pe.wait_ge(rstd_ready, ROUNDS * 4 + START)
            pe.wait_ge(head_normed, ROUNDS * 2 + START)
            with pe.Fori(0, CHUNKS // 2) as two:
                for j in range(2 * C_HALVES):
                    b, k = divmod(j, C_HALVES)
                    slot = j % W_SLOTS
                    if k == 0:
                        pe.wait_ge(out_added, two * (2 * ST) + b * ST + START)
                    if j == C_HALVES:
                        pe.wait_ge(evacuated, ROUNDS * 4 + START)
                        pe.wait_ge(pool_mixed, ROUNDS * 2 + START)
                    if b == 0:
                        pe.wait_ge(m_lo_ready, k + 1)
                    pe.wait_ge(w_hi_ready, two * (2 * C_HALVES) + IN_HALVES + j + 1)
                    pe.wait_ge(w_lo_ready, two * (2 * C_HALVES) + IN_HALVES + j + 1)
                    for t in range(ST):
                        cols = slice(t * P, (t + 1) * P)
                        last = products(ps[:, OUT_BANKS[b][t], :],
                                        [(h_hi[:, k, cols], w_hi[:, slot, :]), (h_lo[:, k, cols], w_hi[:, slot, :]),
                                         (h_hi[:, k, cols], w_lo[:, slot, :])], k == 0, k == KT - 1)
                        if k == KT - 1 and t < ST - 1:
                            last.then_inc(out_tile_done, 1)
                    last.then_inc(w_used, 1)

        @block.scalar
        def _(act):
            act.dma_start(norm_source, norm_w).then_inc(norm_row_in, 16)
            act.dma_start(ident[:, :], identity).then_inc(ident_in, 16)
            nc.scalar.preload_act_table(ACT.Sqrt)
            for started in (evacuated, rstd_ready):
                act.sem_inc(started, START)
            act.wait_ge(setup_step, 1)
            def x_high(t, b):
                act.wait_ge(x_transposed, 2 * t + b + 1)
                bank = 4 * (t % 2) + 2 * b
                nc.scalar.copy(h_hi[:, 8 * b:8 * b + 8, t * P:(t + 1) * P],
                               ps[:, bank:bank + 2, :].rearrange("p b (k s) -> p (b k) s", s=P)
                               ).then_inc(h_hi_ready, 1)

            def x_stats(t):
                act.wait_ge(x_in[t], 16)
                nc.scalar.activation(at_hi[:, :, :].rearrange("p t n -> p (t n)"), x_rows[:, t, :], ACT.Square,
                                     accum_out=x_ss[:, t:t + 1]).then_inc(x_squared, 1)
                act.wait_ge(x_squared, t + 1)
                nc.scalar.activation(x_rms[:, t:t + 1], x_ss[:, t:t + 1], ACT.Sqrt, bias=eps_t[:, :],
                                     scale=1.0 / D).then_inc(x_rms_ready, 1)

            def split_high(h, rnd, base=0, rounds=HALVES):
                unit, part = divmod(h, 2)
                if part == 0:
                    act.wait_ge(raw_in[unit % RAW_SLOTS],
                                (rnd * (rounds // 2 // RAW_SLOTS) + (base // 2 + unit) // RAW_SLOTS + 1) * 16)
                if h >= W_SLOTS or base:
                    act.wait_ge(w_used, rnd * rounds + base + h - W_SLOTS + 1)
                nc.scalar.copy(w_hi[:, h % W_SLOTS, :], raw[:, unit % RAW_SLOTS, part * 512:part * 512 + 512]
                               ).then_inc(w_hi_ready, 1)

            x_stats(0)
            x_stats(1)
            for t in range(ST):
                x_high(t, 0)
                if t + 2 < ST:
                    x_stats(t + 2)
                x_high(t, 1)
                if t == ST - 2:
                    split_high(0, 0)
                    split_high(1, 0)
            for h in range(2, W_SLOTS):
                split_high(h, 0)
            act.wait_ge(lam_summed, 1)
            nc.scalar.activation(lam_exp[:, :], lam_sum[:, :], ACT.Exp).then_inc(lam_exped, 1)

            def rstd(dst, src, width, count):
                act.wait_ge(squares_summed, count)
                nc.scalar.activation(dst, src, ACT.Ln, bias=eps_t[:, :], scale=1.0 / width).then_inc(log_ready, 1)
                act.wait_ge(log_ready, count)
                nc.scalar.activation(dst, dst, ACT.Exp, scale=-0.5).then_inc(rstd_ready, 1)

            def squares(full, high, src):
                nc.scalar.activation(full, src, ACT.Square).then_inc(squares_ready, 1)
                nc.scalar.activation(high, src, ACT.Square).then_inc(squares_ready, 1)

            def mixed_high(k):
                act.wait_ge(w_used, IN_HALVES - G_HALVES + k // 2 + 1)
                if k < 8:
                    act.wait_ge(head_mixed, k + 1 + START)
                else:
                    act.wait_ge(pool_mixed, k - 7 + START)
                nc.scalar.copy(h_hi[:, k, :], mixed[:, k * SEQ:(k + 1) * SEQ]).then_inc(m_hi_ready, 1)

            def act_round(r, last_round=False):
                for m in range(1, HALVES + 1):
                    if m in (8, 16):
                        n = m // 8 - 1
                        if n == 0:
                            nc.scalar.preload_act_table_set(LN_EXP)
                        act.wait_ge(w_used, r * HALVES + m)
                        if n == 0:
                            act.wait_ge(pool_mixed, r * 2 + START)
                        squares(wk(3 * n), sq_hi, ps[:, 2 * n:2 * n + 2, :])
                    if m in (10, 18):
                        n = int(m == 18)
                        rstd(wk(3 * n), ps[:, S0:S0 + 2, :], HEAD_DIM, r * 4 + n + 1)
                        if n == 0:
                            act.wait_ge(rstd_ready, r * 4 + 1 + START)
                            nc.scalar.activation(wk(1), wk(0), ACT.Square).then_inc(rstd_squared, 1)
                    if m in (17, 22):
                        n = int(m == 22)
                        act.wait_ge(qk_rotated, r * 2 + n + 1)
                        for c in range(2):
                            rows = slice(64 * c, 64 * c + 64)
                            nc.scalar.copy((kh_twice, q_stack)[n][rows, c], wk(0)[rows]).then_inc(qk_hi_ready, 1)
                    split_high(m + 3, r)
                    if m == 4:
                        act.wait_ge(wp_lo_ready, r + START)
                        act.wait_ge(pool_mixed, r * 2 + START)
                        act.dma_start(wp_raw[:, :].rearrange("p (k n) -> p k n", k=2),
                                      w_pool[:, bass.ds(r * 2, 2), :]).then_inc(wp_in, 16)
                        act.dma_start(inv_cnt[:, :], inv_count[bass.ds(r, 1), :].to_broadcast([P, SEQ])
                                      ).then_inc(inv_in, 16)
                        act.dma_start(p_scale[:, :], pool_scale[:, bass.ds(r * 2, 2)]).then_inc(scale_in, 16)
                    if m == 24:
                        act.wait_ge(w_used, r * HALVES + 24)
                        act.wait_ge(diff_lo_ready, r + START)
                        nc.scalar.copy(wk(4), ps[:, 0:2, :]).then_inc(evacuated, 1)
                    if m == 26:
                        act.wait_ge(q_moved, r * 32 + 32)
                        for h in range(2):
                            act.wait_ge(v_transposed, r * 2 + h + 1)
                            nc.scalar.copy(v_hi[:, h, :], ps[:, TB + h, :]).then_inc(v_hi_ready, 1)
                    if m == 33:
                        nc.scalar.preload_act_table(ACT.Silu)
                        act.wait_ge(w_used, r * HALVES + 32)
                        act.wait_ge(head_mixed, r * 2 + START)
                        nc.scalar.activation(gate[:, :, :], ps[:, 2:4, :], ACT.Silu).then_inc(evacuated, 1)
                        nc.scalar.preload_act_table_set(LN_EXP)
                    i, odd = divmod(m - 26, 2)
                    if 0 <= i <= ITEMS and not odd:
                        if i >= 1:
                            act.wait_ge(at_transposed, r * ITEMS + i)
                            if i - 1 == ST:
                                act.wait_ge(head_done, r * 2 + 1)
                            t = (i - 1) % ST
                            nc.scalar.copy(at_hi[:, :, t * P:(t + 1) * P],
                                           ps[:, TB, :].rearrange("p (t s) -> p t s", t=ST)
                                           ).then_inc(at_hi_ready, 1)
                        if i < ITEMS:
                            act.wait_ge(max_ready, r * ITEMS + i + 1)
                            for c in range(2):
                                nc.scalar.activation(probs[:, c, :], ps[:, S0 + c, :], ACT.Exp,
                                                     bias=neg_max[:, c:c + 1], scale=SCALE,
                                                     accum_out=row_sum[:, c:c + 1]).then_inc(exp_done, 1)
                    if m in (39, 44):
                        h = int(m == 44)
                        act.wait_ge(head_done, r * 2 + h + 1)
                        act.wait_ge(head_mixed, r * 2 + h + START)
                        act.wait_ge(scored, r * ITEMS + ITEMS)
                        squares(head_out[:, :], hsq_hi, ps[:, OB, :])
                    if m == 41:
                        act.wait_ge(wp_in, r * 16 + 16)
                        nc.scalar.copy(wp_hi, wp_raw[:, :]).then_inc(wp_hi_ready, 1)
                    if m == 40:
                        act.wait_ge(w_used, r * HALVES + 40)
                        act.wait_ge(q_low_ready, r * 2 + 2)
                        nc.scalar.copy(wk(0), ps[:, 0:2, :]).then_inc(evacuated, 1)
                    if m == 42:
                        rstd(head_out[:, :], ps[:, S0, :], 2 * HEAD_DIM, r * 4 + 3)
                    if m == 46:
                        act.wait_ge(diff_ready, r + 1)
                        nc.scalar.copy(diff_hi, wk(4)).then_inc(diff_hi_ready, 1)
                        rstd(head_out[:, :], ps[:, TB, :], 2 * HEAD_DIM, r * 4 + 4)
                        nc.scalar.preload_act_table(ACT.Silu)
                    if m == 48:
                        act.wait_ge(w_used, r * HALVES + HALVES)
                        nc.scalar.activation(wk(0), ps[:, 2:4, :], ACT.Silu).then_inc(evacuated, 1)
                    if last_round and 44 <= m < 48:
                        mixed_high(m - 44)

            with act.Fori(0, ROUNDS - 1) as r:
                act_round(r)
            act_round(ROUNDS - 1, last_round=True)

            for h in range(W_SLOTS, CHUNKS * C_HALVES):
                if h < KT:
                    mixed_high(h)
                split_high(h, 0, IN_HALVES)

        @block.vector
        def _(dve):
            steps = [0]

            def setup(ins):
                steps[0] += 1
                ins.then_inc(setup_step, 1)
                dve.wait_ge(setup_step, steps[0])

            setup(nc.vector.memset(eps_t[:, :], EPS))
            dve.sem_inc(out_added, CREDIT)
            for started in (head_normed, head_mixed, pool_mixed, wp_lo_ready, diff_lo_ready):
                dve.sem_inc(started, START)

            def x_low(t, b):
                dve.wait_ge(h_hi_ready, 2 * t + b + 1)
                bank = 4 * (t % 2) + 2 * b
                nc.vector.tensor_tensor(h_lo[:, 8 * b:8 * b + 8, t * P:(t + 1) * P],
                                        ps[:, bank:bank + 2, :].rearrange("p b (k s) -> p (b k) s", s=P),
                                        h_hi[:, 8 * b:8 * b + 8, t * P:(t + 1) * P].bitcast(F32), ALU.subtract
                                        ).then_inc(h_lo_ready, 1)

            dve.wait_ge(norm_spread, 1)

            def x_norm(t):
                dve.wait_ge(x_rms_ready, t + 1)
                setup(nc.vector.reciprocal(x_rstd[:, t:t + 1], x_rms[:, t:t + 1]))
                nc.vector.scalar_tensor_tensor(out=x_rows[:, t, :], in0=x_rows[:, t, :], scalar=x_rstd[:, t:t + 1],
                                               in1=norm_row, op0=ALU.mult, op1=ALU.mult).then_inc(x_normed, 1)

            def split_low(h, rnd, base=0, rounds=HALVES):
                unit, part = divmod(h, 2)
                dve.wait_ge(w_hi_ready, rnd * rounds + base + h + 1)
                nc.vector.tensor_tensor(w_lo[:, h % W_SLOTS, :],
                                        raw[:, unit % RAW_SLOTS, part * 512:part * 512 + 512],
                                        w_hi[:, h % W_SLOTS, :].bitcast(F32), ALU.subtract).then_inc(w_lo_ready, 1)

            x_norm(0)
            x_norm(1)
            for t in range(ST):
                x_low(t, 0)
                if t + 2 < ST:
                    x_norm(t + 2)
                if t == ST - 1:
                    split_low(0, 0)
                x_low(t, 1)
            for h in range(1, W_SLOTS):
                split_low(h, 0)
            dve.wait_ge(x_normed, ST)
            setup(nc.vector.memset(wk_cols(0, 0, PAD), 0.0))
            setup(nc.vector.memset(wk_cols(0, PAD + SEQ, XW), 0.0))
            dve.wait_ge(lam_loaded, 64)
            setup(nc.vector.tensor_tensor(lam_prod[:, :, :], lam_in[:, 0:2, :], lam_in[:, 2:4, :], ALU.mult))
            nc.vector.reduce_sum(lam_sum[:, :], lam_prod[:, :, :], AX_X).then_inc(lam_summed, 1)
            dve.wait_ge(const_in, CONSTS * 16)
            setup(nc.vector.tensor_scalar(sw[:, :], sw[:, :], 1.0 - LAMBDA_INIT, None, ALU.mult))
            setup(nc.vector.tensor_copy(ones_pair_r[:, :], ones_pair[:, :]))
            setup(nc.vector.memset(ones_all_r[:, :].bitcast(F32), 1.0))
            dve.wait_ge(lam_exped, 1)
            setup(nc.vector.tensor_tensor(neg_lam[:, :], lam_exp[:, 1:2], lam_exp[:, 0:1], ALU.subtract))
            setup(nc.vector.tensor_scalar(neg_lam[:, :], neg_lam[:, :], LAMBDA_INIT, None, ALU.subtract))

            def mixed_low(k):
                dve.wait_ge(m_hi_ready, k + 1)
                nc.vector.tensor_tensor(h_lo[:, k, :], mixed[:, k * SEQ:(k + 1) * SEQ],
                                        h_hi[:, k, :].bitcast(F32), ALU.subtract).then_inc(m_lo_ready, 1)

            def dve_round(r, last_round=False):
                step = [0]

                def chain(ins):
                    step[0] += 1
                    ins.then_inc(dve_step, 1)
                    dve.wait_ge(dve_step, r * STEPS + step[0])

                for m in range(1, HALVES + 1):
                    if m in (9, 17):
                        n = (m - 9) // 8
                        dve.wait_ge(squares_ready, r * 8 + 2 * n + 2)
                        nc.vector.tensor_tensor(sq_lo, wk(3 * n), sq_hi.bitcast(F32), ALU.subtract
                                                ).then_inc(squares_low_ready, 1)
                    if m == 11:
                        dve.wait_ge(rstd_squared, r + 1)
                        chain(nc.vector.scalar_tensor_tensor(
                            out=wk(1), in0=ps[:, S0:S0 + 2, :], scalar=HEAD_DIM * EPS, in1=wk(1),
                            op0=ALU.add, op1=ALU.mult))
                        chain(nc.vector.tensor_scalar(wk(1), wk(1), -0.5 / HEAD_DIM, 1.5, ALU.mult, ALU.add))
                    if m in (12, 19):
                        n = int(m == 19)
                        if n == 0:
                            chain(nc.vector.tensor_tensor(wk(0), wk(0), wk(1), ALU.mult))
                        else:
                            dve.wait_ge(k_low_ready, r * 2 + 2)
                            dve.wait_ge(rstd_ready, r * 4 + 2 + START)
                        nc.vector.scalar_tensor_tensor(out=wk(0), in0=ps[:, 2 * n:2 * n + 2, :],
                                                       scalar=(kw, qw)[n][:, :], in1=wk(3 * n),
                                                       op0=ALU.mult, op1=ALU.mult).then_inc(qk_normed, 1)
                        dve.wait_ge(qk_normed, r * 2 + n + 1)
                    if m in (13, 19):
                        nc.vector.tensor_tensor(wk(2), wk(0), twice(cos_t), ALU.mult)
                        chain(nc.vector.stream_shuffle(wk(1), wk(0), ROPE_PARTNER))
                    if m in (15, 20):
                        chain(nc.vector.tensor_tensor(wk(1), wk(1), twice(sin_t), ALU.mult))
                    if m in (16, 20):
                        nc.vector.tensor_tensor(wk(0), wk(2), wk(1), ALU.add).then_inc(qk_rotated, 1)
                    if m in (18, 22):
                        n = int(m == 22)
                        for c in range(2):
                            rows = slice(64 * c, 64 * c + 64)
                            dve.wait_ge(qk_hi_ready, r * 4 + 2 * n + c + 1)
                            nc.vector.tensor_tensor(q_low[rows] if n else kl_twice[rows, c], wk(0)[rows],
                                                    (kh_twice, q_stack)[n][rows, c].bitcast(F32), ALU.subtract
                                                    ).then_inc((k_low_ready, q_low_ready)[n], 1)
                    i, odd = divmod(m - 25, 2)
                    if 1 <= i <= ITEMS and not odd:
                        dve.wait_ge(exp_done, r * (2 * ITEMS) + 2 * i)
                        chain(nc.vector.reciprocal(row_inv[:, :], row_sum[:, :]))
                        nc.vector.tensor_tensor(coef[:, :], row_inv[:, 1:2], neg_lam[:, :], ALU.mult)
                        chain(nc.vector.tensor_scalar(probs[:, 0, :], probs[:, 0, :], row_inv[:, 0:1], None,
                                                      ALU.mult))
                        nc.vector.scalar_tensor_tensor(out=probs[:, 0, :], in0=probs[:, 1, :],
                                                       scalar=coef[:, :], in1=probs[:, 0, :],
                                                       op0=ALU.mult, op1=ALU.add).then_inc(attn_ready, 1)
                    split_low(m + 3, r)
                    if m in (40, 45):
                        h = int(m == 45)
                        dve.wait_ge(squares_ready, r * 8 + 2 * h + 6)
                        nc.vector.tensor_tensor(hsq_lo, head_out[:, :], hsq_hi.bitcast(F32), ALU.subtract
                                                ).then_inc(squares_low_ready, 1)
                    if 0 <= i < ITEMS and not odd:
                        dve.wait_ge(scored, r * ITEMS + i + 1)
                        chain(nc.vector.reduce_max(row_max[:, :], ps[:, S0:S0 + 2, :], AX_X))
                        nc.vector.tensor_scalar(neg_max[:, :], row_max[:, :], -SCALE, None, ALU.mult
                                                ).then_inc(max_ready, 1)
                    if odd and 1 <= i <= ITEMS:
                        dve.wait_ge(at_hi_ready, r * ITEMS + i)
                        t = (i - 1) % ST
                        nc.vector.tensor_tensor(at_lo[:, :, t * P:(t + 1) * P],
                                                ps[:, TB, :].rearrange("p (t s) -> p t s", t=ST),
                                                at_hi[:, :, t * P:(t + 1) * P].bitcast(F32), ALU.subtract
                                                ).then_inc(at_lo_ready, 1)
                    if m == 26:
                        for h in range(2):
                            dve.wait_ge(v_hi_ready, r * 2 + h + 1)
                            nc.vector.tensor_tensor(v_lo[:, h, :], ps[:, TB + h, :], v_hi[:, h, :].bitcast(F32),
                                                    ALU.subtract).then_inc(v_lo_ready, 1)
                    if m == 42:
                        dve.wait_ge(wp_hi_ready, r + 1)
                        nc.vector.tensor_tensor(wp_lo, wp_raw[:, :], wp_hi.bitcast(F32),
                                                ALU.subtract).then_inc(wp_lo_ready, 1)
                    if m == 41:
                        dve.wait_ge(evacuated, r * 4 + 3 + START)
                        chain(nc.vector.tensor_tensor(wk_cols(1, 1, 527), wk_cols(0, 0, 526), wk_cols(0, 1, 527),
                                                      ALU.add))
                    if m in (43, 47):
                        h = int(m == 47)
                        dve.wait_ge(rstd_ready, r * 4 + 3 + h + START)
                        nc.vector.scalar_tensor_tensor(out=head_out[:, :], in0=ps[:, OB, :], scalar=sw[:, :],
                                                       in1=head_out[:, :], op0=ALU.mult, op1=ALU.mult
                                                       ).then_inc(head_normed, 1)
                        dve.wait_ge(head_normed, r * 2 + h + 1 + START)
                        nc.vector.tensor_tensor(mixed[:, bass.ds(r * (2 * SEQ) + h * SEQ, SEQ)], head_out[:, :],
                                                gate[:, h, :], ALU.mult).then_inc(head_mixed, 1)
                    if m == 43:
                        chain(nc.vector.tensor_tensor(wk_cols(2, 2, 526), wk_cols(1, 1, 525), wk_cols(1, 3, 527),
                                                      ALU.add))
                        chain(nc.vector.tensor_tensor(wk_cols(3, 4, 524), wk_cols(2, 2, 522), wk_cols(2, 6, 526),
                                                      ALU.add))
                    if m == 44:
                        chain(nc.vector.tensor_tensor(wk(4), wk_cols(3, 4, 516), wk_cols(3, 12, 524), ALU.add))
                    if m == 45:
                        dve.wait_ge(inv_in, r * 16 + 16)
                        chosen = work[:, bass.ds(r * (2 * XW) + 2 * XW, 2 * XW)].rearrange(
                            "p (c n) -> p c n", c=2)[:, :, PAD:PAD + SEQ]
                        chain(nc.vector.tensor_tensor(wk(4), chosen, twice(inv_cnt), ALU.mult))
                        nc.vector.tensor_tensor(wk(4), wk(4), wk(0), ALU.subtract).then_inc(diff_ready, 1)
                    if m == 46:
                        dve.wait_ge(diff_hi_ready, r + 1)
                        nc.vector.tensor_tensor(diff_lo, wk(4), diff_hi.bitcast(F32), ALU.subtract
                                                ).then_inc(diff_lo_ready, 1)
                    if m == 48:
                        dve.wait_ge(pool_done, r + 1)
                        dve.wait_ge(scale_in, r * 16 + 16)
                        dve.wait_ge(evacuated, r * 4 + 4 + START)
                        for c in range(2):
                            nc.vector.scalar_tensor_tensor(
                                out=mixed[:, bass.ds(r * (2 * SEQ) + (8 + c) * SEQ, SEQ)], in0=ps[:, S0 + c, :],
                                scalar=p_scale[:, c:c + 1], in1=wk(0)[:, c, :], op0=ALU.mult, op1=ALU.mult
                            ).then_inc(pool_mixed, 1)
                    if last_round and 44 <= m < 48:
                        mixed_low(m - 44)
                assert step[0] == STEPS, step[0]

            with dve.Fori(0, ROUNDS - 1) as r:
                dve_round(r)
            dve_round(ROUNDS - 1, last_round=True)

            def add_x(chunk):
                dve.wait_ge(res_in[chunk], 16)
                for t in range(ST):
                    if t < ST - 1:
                        dve.wait_ge(out_tile_done, (ST - 1) * chunk + t + 1)
                    else:
                        dve.wait_ge(w_used, IN_HALVES + C_HALVES * (chunk + 1))
                    tile = mixed[:, (ST * chunk + t) * SEQ:(ST * chunk + t + 1) * SEQ]
                    nc.vector.tensor_tensor(tile, ps[:, OUT_BANKS[chunk % 2][t], :], tile, ALU.add
                                            ).then_inc(out_added, 1)

            for h in range(W_SLOTS, CHUNKS * C_HALVES):
                if h < KT:
                    mixed_low(h)
                split_low(h, 0, IN_HALVES)
                if h % C_HALVES == 3 and h > C_HALVES:
                    add_x(h // C_HALVES - 1)
            add_x(CHUNKS - 1)


CONSTS = 8
LN_EXP = "natural_log_exp_and_others"
STEPS = 36
ROPE_PARTNER = list(range(8, 16)) + list(range(0, 8)) + list(range(16, 32))


def x_rows_of(mixed, chunk, tiles, width):
    return mixed[:, chunk * tiles * width:(chunk + 1) * tiles * width].rearrange("p (t n) -> p t n", t=tiles)


def kernel(x, norm_w, w_in, q_norm_w, k_norm_w, lambda_q1, lambda_k1, lambda_q2, lambda_k2, subln_w,
           w_pool, pool_scale, w_out):
    import numpy as np
    import concourse.bacc as bacc
    from concourse.bass_utils import run_bass_kernel_spmd

    f = np.float32
    seq, d = x.shape[1], x.shape[2]
    identity = np.eye(P, dtype=f)
    pair_ones = np.kron(np.eye(2, dtype=f), np.ones((HEAD_DIM, HEAD_DIM), f))
    half = HEAD_DIM // 8
    inv_freq = (500000.0 ** (-np.arange(0, 2 * half, 2, dtype=np.float64) / (2 * half))).astype(f)
    ang = np.arange(seq, dtype=f)[None, :] * inv_freq[:, None]
    cos, sin = np.cos(ang.astype(np.float64)).astype(f), np.sin(ang.astype(np.float64)).astype(f)
    rope_cos, rope_sin = np.ones((P, seq), f), np.zeros((P, seq), f)
    for c in (0, HEAD_DIM):
        rope_cos[c:c + half], rope_cos[c + half:c + 2 * half] = cos, cos
        rope_sin[c:c + half], rope_sin[c + half:c + 2 * half] = -sin, sin
    pos = np.arange(seq)
    inv_count = np.stack([1.0 / (np.minimum(pos + w - 1 - w // 2, seq - 1) - np.maximum(pos - w // 2, 0) + 1)
                          for w in (2, 4, 8, 16)]).astype(f)
    tiled = w_pool[0].shape[1] // P
    arrays = {
        "x": x[0], "norm_w": norm_w, "w_in": w_in[0], "q_norm_w": np.reshape(q_norm_w, (-1, 1)),
        "k_norm_w": np.reshape(k_norm_w, (-1, 1)), "lq1": lambda_q1, "lk1": lambda_k1, "lq2": lambda_q2,
        "lk2": lambda_k2, "subln_w": np.reshape(subln_w, (-1, 1)),
        "w_pool": np.reshape(np.transpose(np.reshape(w_pool[0], (-1, P, w_pool.shape[3])), (1, 0, 2)),
                             (P, N_WINDOWS * tiled, w_pool.shape[3])),
        "pool_scale": np.transpose(np.reshape(pool_scale, (-1, P))), "w_out": w_out[0],
        "identity": identity, "pair_ones": pair_ones, "rope_cos": rope_cos, "rope_sin": rope_sin,
        "inv_count": inv_count,
    }
    arrays = {n: np.ascontiguousarray(a) for n, a in arrays.items()}
    nc = bacc.Bacc("TRN2", target_bir_lowering=False, num_devices=1, dynamic_dma_scratch_size=2048)
    args = [nc.dram_tensor(f"in_{n}", a.shape, mybir.dt.from_np(a.dtype), kind="ExternalInput").ap()
            for n, a in arrays.items()]
    out = nc.dram_tensor("out", (seq, d), F32, kind="ExternalOutput").ap()
    hybrid_block(nc, *args, out)
    r = run_bass_kernel_spmd(nc, [{f"in_{n}": a for n, a in arrays.items()}], core_ids=[0])
    return r.results[0]["out"].reshape(1, seq, d)
```
